# Optimizing a Trainium2 kernel written in Bass

```python
import math
import jax, jax.numpy as jnp
from jax import lax
import numpy as np

D_MODEL = 1024
BATCH = 1
SEQ = 1024
DEPTH = 1
DEC_BATCH = 8
DEC_SEQ = 4
PAST_LEN = 8192
PAGE_SIZE = 128

EPS = 1e-6
R_WIDTH = D_MODEL
R_HEAD = 64
R_HEADS = R_WIDTH // R_HEAD
R_DECAY_LORA = 64
R_AAA_LORA = 64
R_GATE_LORA = 128
R_COLS = 3 * R_WIDTH + R_DECAY_LORA + R_AAA_LORA + R_GATE_LORA
R_LN_EPS = 64e-5
S5_WIDTH = D_MODEL
S5_GROUP = 16
S5_GROUPS = S5_WIDTH // S5_GROUP
S5_STATE = 64
M_WIDTH = 2 * D_MODEL
M_HEAD = 64
M_HEADS = M_WIDTH // M_HEAD
M_GROUPS = 4
M_HPG = M_HEADS // M_GROUPS
M_STATE = 128
M_CONV = 4
M_CONV_DIM = M_WIDTH + 2 * M_GROUPS * M_STATE
SSD_CHUNK = 128
MEM_LEN = 256
XA_HEADS = 4
XA_HEAD_DIM = D_MODEL // XA_HEADS
D_FF = 4 * D_MODEL
N_BRANCH = 3
IN_SIZES = (N_BRANCH * D_MODEL, R_COLS, S5_WIDTH, M_WIDTH, M_CONV_DIM, M_HEADS)
IN_COLS = sum(IN_SIZES)

kernel_name = 'hybrid_rwkv7_s5_ssd_memxattn_step'

def split_cols(x, sizes):
    idx = np.cumsum(sizes)[:-1].tolist()
    return jnp.split(x, idx, axis=-1)

def rmsnorm(x, g):
    x32 = x.astype(jnp.float32)
    return x32 * lax.rsqrt(jnp.mean(x32 * x32, axis=-1, keepdims=True) + EPS) * g.astype(jnp.float32)

def rwkv7_recurrence(r, w, k, v, a, b, s0):
    def step(s, inp):
        r_t, w_t, k_t, v_t, a_t, b_t = inp
        sa = jnp.einsum('bhij,bhj->bhi', s, a_t)
        s = s * w_t[:, :, None, :] + sa[..., None] * b_t[:, :, None, :] + v_t[..., None] * k_t[:, :, None, :]
        return s, jnp.einsum('bhij,bhj->bhi', s, r_t)
    xs = [jnp.moveaxis(z.astype(jnp.float32), 1, 0) for z in (r, w, k, v, a, b)]
    s_fin, y = lax.scan(step, s0.astype(jnp.float32), xs)
    return jnp.moveaxis(y, 0, 1), s_fin

def rwkv7_branch(p, shift_prev, s0, mu, w0, w2, a0, a2, g2, k_k, k_a, r_k, ln_w, ln_b, w_out):
    bsz, t, _ = p.shape
    prev = jnp.concatenate([shift_prev[:, None].astype(p.dtype), p[:, :-1]], axis=1)
    pm = p + mu * (prev - p)
    r, k, v, xw, xa, xg = split_cols(pm, (R_WIDTH, R_WIDTH, R_WIDTH, R_DECAY_LORA, R_AAA_LORA, R_GATE_LORA))
    w_log = -jax.nn.softplus(-(w0 + jnp.tanh(xw) @ w2)) - 0.5
    decay = jnp.exp(-jnp.exp(w_log.astype(jnp.float32)))
    a = jax.nn.sigmoid(a0 + xa @ a2)
    g = jax.nn.sigmoid(xg) @ g2
    heads = lambda z: z.reshape(bsz, t, R_HEADS, R_HEAD)
    kk = heads((k * k_k).astype(jnp.float32))
    kk = kk * lax.rsqrt(jnp.sum(kk * kk, axis=-1, keepdims=True) + 1e-12)
    k = k * (1.0 + (a - 1.0) * k_a)
    rh, kh, vh, ah = heads(r), heads(k), heads(v), heads(a)
    y, s_fin = rwkv7_recurrence(rh, heads(decay), kh, vh, -kk, kk * ah, s0)
    mean = jnp.mean(y, axis=-1, keepdims=True)
    var = jnp.mean(jnp.square(y - mean), axis=-1, keepdims=True)
    y = ((y - mean) * lax.rsqrt(var + R_LN_EPS)).reshape(bsz, t, R_WIDTH) * ln_w + ln_b
    bonus = jnp.sum(rh * kh * r_k, axis=-1, keepdims=True) * vh
    y = y + bonus.reshape(bsz, t, R_WIDTH)
    return (y * g) @ w_out, p[:, -1], s_fin

def s5_branch(u, h_re0, h_im0, a_re, a_im, log_dt, b_re, b_im, c_re, c_im, d, w_glu, w_out):
    bsz, t, _ = u.shape
    u32 = u.astype(jnp.float32)
    dt = jnp.exp(log_dt.astype(jnp.float32))[:, None]
    a_re = a_re.astype(jnp.float32)
    a_im = a_im.astype(jnp.float32)
    mag = jnp.exp(dt * a_re)
    abar_re = mag * jnp.cos(dt * a_im)
    abar_im = mag * jnp.sin(dt * a_im)
    den = a_re * a_re + a_im * a_im
    nr = abar_re - 1.0
    q_re = (nr * a_re + abar_im * a_im) / den
    q_im = (abar_im * a_re - nr * a_im) / den
    bb_re = q_re[..., None] * b_re - q_im[..., None] * b_im
    bb_im = q_re[..., None] * b_im + q_im[..., None] * b_re
    ug = u32.reshape(bsz, t, S5_GROUPS, S5_GROUP)
    in_re = jnp.einsum('btgh,gph->btgp', ug, bb_re)
    in_im = jnp.einsum('btgh,gph->btgp', ug, bb_im)
    in_re = in_re.at[:, 0].add(abar_re * h_re0 - abar_im * h_im0)
    in_im = in_im.at[:, 0].add(abar_re * h_im0 + abar_im * h_re0)
    ar_t = jnp.broadcast_to(abar_re, (1, t, S5_GROUPS, S5_STATE))
    ai_t = jnp.broadcast_to(abar_im, (1, t, S5_GROUPS, S5_STATE))

    def combine(e1, e2):
        a1r, a1i, b1r, b1i = e1
        a2r, a2i, b2r, b2i = e2
        return (a2r * a1r - a2i * a1i, a2r * a1i + a2i * a1r,
                a2r * b1r - a2i * b1i + b2r, a2r * b1i + a2i * b1r + b2i)

    _, _, h_re, h_im = lax.associative_scan(combine, (ar_t, ai_t, in_re, in_im), axis=1)
    y = jnp.einsum('btgp,ghp->btgh', h_re, c_re) - jnp.einsum('btgp,ghp->btgh', h_im, c_im)
    y = y.reshape(bsz, t, S5_WIDTH) + d * u32
    y = jax.nn.gelu(y)
    y = y * jax.nn.sigmoid(y @ w_glu)
    return y @ w_out, h_re[:, -1], h_im[:, -1]

def ssd_chunked(x, dt, a, bm, cm, h0):
    bsz, t = x.shape[:2]
    chunk = SSD_CHUNK if t % SSD_CHUNK == 0 else t
    nc = t // chunk
    xd = (x * dt[..., None]).reshape(bsz, nc, chunk, M_GROUPS, M_HPG, M_HEAD)
    adt = (dt * a).reshape(bsz, nc, chunk, M_GROUPS, M_HPG)
    bm = bm.reshape(bsz, nc, chunk, M_GROUPS, M_STATE)
    cm = cm.reshape(bsz, nc, chunk, M_GROUPS, M_STATE)
    a_cum = jnp.cumsum(adt, axis=2)
    causal = jnp.tril(jnp.ones((chunk, chunk), dtype=bool))[None, None, :, :, None, None]
    seg = a_cum[:, :, :, None] - a_cum[:, :, None, :]
    decay_ls = jnp.exp(jnp.where(causal, seg, -jnp.inf))
    y_diag = jnp.einsum('bclgn,bcsgn,bclsge,bcsgep->bclgep', cm, bm, decay_ls, xd)
    decay_to_end = jnp.exp(a_cum[:, :, -1:] - a_cum)
    chunk_states = jnp.einsum('bclgn,bclge,bclgep->bcgepn', bm, decay_to_end, xd)
    chunk_decay = jnp.exp(a_cum[:, :, -1])

    def carry_step(h, inp):
        dec_c, st_c = inp
        return h * dec_c[..., None, None] + st_c, h

    h_fin, h_start = lax.scan(carry_step, h0.astype(jnp.float32),
                              (jnp.moveaxis(chunk_decay, 1, 0), jnp.moveaxis(chunk_states, 1, 0)))
    h_start = jnp.moveaxis(h_start, 0, 1)
    y_off = jnp.einsum('bclgn,bcgepn,bclge->bclgep', cm, h_start, jnp.exp(a_cum))
    return (y_diag + y_off).reshape(bsz, t, M_GROUPS, M_HPG, M_HEAD), h_fin

def mamba2_branch(z, xbc, dt_raw, conv_prev, h0, conv_w, conv_b, dt_bias, a_log, d_skip, norm_g, w_out):
    bsz, t, _ = xbc.shape
    padded = jnp.concatenate([conv_prev.astype(jnp.float32), xbc.astype(jnp.float32)], axis=1)
    conv = conv_b + padded[:, 0:t] * conv_w[0]
    for j in range(1, M_CONV):
        conv = conv + padded[:, j:j + t] * conv_w[j]
    conv = jax.nn.silu(conv)
    xs, bm, cm = split_cols(conv, (M_WIDTH, M_GROUPS * M_STATE, M_GROUPS * M_STATE))
    dt = jax.nn.softplus(dt_raw.astype(jnp.float32) + dt_bias)
    a = -jnp.exp(a_log.astype(jnp.float32))
    xh = xs.reshape(bsz, t, M_GROUPS, M_HPG, M_HEAD)
    y, h_fin = ssd_chunked(xh, dt.reshape(bsz, t, M_GROUPS, M_HPG), a.reshape(M_GROUPS, M_HPG),
                           bm.reshape(bsz, t, M_GROUPS, M_STATE), cm.reshape(bsz, t, M_GROUPS, M_STATE),
                           h0.reshape(bsz, M_GROUPS, M_HPG, M_HEAD, M_STATE))
    y = y + d_skip.reshape(M_GROUPS, M_HPG)[..., None] * xh
    y = y.reshape(bsz, t, M_WIDTH) * jax.nn.silu(z)
    yg = y.reshape(bsz, t, M_GROUPS, M_WIDTH // M_GROUPS)
    yg = yg * lax.rsqrt(jnp.mean(yg * yg, axis=-1, keepdims=True) + EPS)
    y = yg.reshape(bsz, t, M_WIDTH) * norm_g
    return y @ w_out, padded[:, t:], h_fin.reshape(bsz, M_HEADS, M_HEAD, M_STATE)

def cross_attend(xn, mem_k, mem_v, w_q, w_o):
    bsz, t, _ = xn.shape
    q = (xn @ w_q).reshape(bsz, t, XA_HEADS, XA_HEAD_DIM)
    s = jnp.einsum('bthd,bmhd->bhtm', q, mem_k).astype(jnp.float32) * (XA_HEAD_DIM ** -0.5)
    p = jax.nn.softmax(s, axis=-1)
    o = jnp.einsum('bhtm,bmhd->bthd', p, mem_v).reshape(bsz, t, D_MODEL)
    return o @ w_o

def setup_inputs(seed: int = 0) -> dict:
    key = jax.random.key(seed)
    keys = jax.random.split(key, 64)
    counter = [0]
    f32 = jnp.float32

    def nk():
        counter[0] += 1
        return keys[counter[0] - 1]

    def nrm(shape, scale=1.0):
        return scale * jax.random.normal(nk(), shape, f32)

    def unif(shape, lo, hi):
        return jax.random.uniform(nk(), shape, f32, lo, hi)

    def gain(shape, s=0.05):
        return 1.0 + nrm(shape, s)

    L, D = DEPTH, D_MODEL
    inp = {}
    inp['x_prompt'] = nrm((BATCH, SEQ, D))
    inp['x_sample'] = nrm((DEC_BATCH, DEC_SEQ, D))
    inp['cache_mem_k'] = nrm((L, DEC_BATCH, MEM_LEN, XA_HEADS, XA_HEAD_DIM))
    inp['cache_mem_v'] = nrm((L, DEC_BATCH, MEM_LEN, XA_HEADS, XA_HEAD_DIM))
    inp['state_rwkv'] = nrm((L, DEC_BATCH, R_HEADS, R_HEAD, R_HEAD), 0.5)
    inp['state_rwkv_shift'] = nrm((L, DEC_BATCH, R_COLS))
    inp['state_s5_re'] = nrm((L, DEC_BATCH, S5_GROUPS, S5_STATE), 0.5)
    inp['state_s5_im'] = nrm((L, DEC_BATCH, S5_GROUPS, S5_STATE), 0.5)
    inp['state_conv'] = nrm((L, DEC_BATCH, M_CONV - 1, M_CONV_DIM))
    inp['state_ssm'] = nrm((L, DEC_BATCH, M_HEADS, M_HEAD, M_STATE), 0.5)
    inp['mem_prompt'] = nrm((BATCH, MEM_LEN, D))
    inp['norm_mix_pre'] = gain((L, D))
    inp['norm_mix_post'] = gain((L, D))
    inp['norm_xa_pre'] = gain((L, D))
    inp['norm_xa_post'] = gain((L, D))
    inp['norm_mlp_pre'] = gain((L, D))
    inp['norm_mlp_post'] = gain((L, D))
    inp['norm_mem'] = gain((L, D))
    inp['w_in'] = nrm((L, D, IN_COLS), D ** -0.5)
    inp['w_out'] = nrm((L, D, D), D ** -0.5)
    inp['rwkv_mu'] = unif((L, R_COLS), 0.0, 1.0)
    inp['rwkv_w0'] = unif((L, R_WIDTH), -6.5, -1.5)
    inp['rwkv_w2'] = nrm((L, R_DECAY_LORA, R_WIDTH), 0.5 * R_DECAY_LORA ** -0.5)
    inp['rwkv_a0'] = nrm((L, R_WIDTH), 0.1)
    inp['rwkv_a2'] = nrm((L, R_AAA_LORA, R_WIDTH), R_AAA_LORA ** -0.5)
    inp['rwkv_g2'] = nrm((L, R_GATE_LORA, R_WIDTH), R_GATE_LORA ** -0.5)
    inp['rwkv_k_k'] = 0.85 + nrm((L, R_WIDTH), 0.05)
    inp['rwkv_k_a'] = gain((L, R_WIDTH))
    inp['rwkv_r_k'] = nrm((L, R_HEADS, R_HEAD), 0.1)
    inp['rwkv_ln_w'] = gain((L, R_WIDTH))
    inp['rwkv_ln_b'] = nrm((L, R_WIDTH), 0.01)
    inp['w_out_rwkv'] = nrm((L, R_WIDTH, D), R_WIDTH ** -0.5)
    inp['s5_a_re'] = -0.5 * jnp.exp(nrm((L, S5_GROUPS, S5_STATE), 0.1))
    inp['s5_a_im'] = math.pi * jnp.arange(S5_STATE, dtype=f32) + nrm((L, S5_GROUPS, S5_STATE), 0.05)
    inp['s5_log_dt'] = unif((L, S5_GROUPS), math.log(1e-3), math.log(1e-1))
    inp['s5_b_re'] = nrm((L, S5_GROUPS, S5_STATE, S5_GROUP), (2 * S5_GROUP) ** -0.5)
    inp['s5_b_im'] = nrm((L, S5_GROUPS, S5_STATE, S5_GROUP), (2 * S5_GROUP) ** -0.5)
    inp['s5_c_re'] = nrm((L, S5_GROUPS, S5_GROUP, S5_STATE), (2 * S5_STATE) ** -0.5)
    inp['s5_c_im'] = nrm((L, S5_GROUPS, S5_GROUP, S5_STATE), (2 * S5_STATE) ** -0.5)
    inp['s5_d'] = nrm((L, S5_WIDTH))
    inp['s5_w_glu'] = nrm((L, S5_WIDTH, S5_WIDTH), S5_WIDTH ** -0.5)
    inp['w_out_s5'] = nrm((L, S5_WIDTH, D), S5_WIDTH ** -0.5)
    inp['m_conv_w'] = nrm((L, M_CONV, M_CONV_DIM), M_CONV ** -0.5)
    inp['m_conv_b'] = nrm((L, M_CONV_DIM), 0.01)
    dt0 = jnp.exp(unif((L, M_HEADS), math.log(1e-3), math.log(1e-1)))
    inp['m_dt_bias'] = dt0 + jnp.log(-jnp.expm1(-dt0))
    inp['m_a_log'] = jnp.log(unif((L, M_HEADS), 1.0, 16.0))
    inp['m_d'] = gain((L, M_HEADS), 0.1)
    inp['m_norm'] = gain((L, M_WIDTH))
    inp['w_out_mamba'] = nrm((L, M_WIDTH, D), M_WIDTH ** -0.5)
    inp['xa_wq'] = nrm((L, D, D), D ** -0.5)
    inp['xa_wk'] = nrm((L, D, D), D ** -0.5)
    inp['xa_wv'] = nrm((L, D, D), D ** -0.5)
    inp['xa_wo'] = nrm((L, D, D), D ** -0.5)
    inp['mlp_w1'] = nrm((L, D, D_FF), D ** -0.5)
    inp['mlp_w2'] = nrm((L, D_FF, D), D_FF ** -0.5)
    return inp

def reference(x_prompt, x_sample, cache_mem_k, cache_mem_v, state_rwkv, state_rwkv_shift,
              state_s5_re, state_s5_im, state_conv, state_ssm, mem_prompt,
              norm_mix_pre, norm_mix_post, norm_xa_pre, norm_xa_post, norm_mlp_pre, norm_mlp_post, norm_mem,
              w_in, w_out,
              rwkv_mu, rwkv_w0, rwkv_w2, rwkv_a0, rwkv_a2, rwkv_g2, rwkv_k_k, rwkv_k_a, rwkv_r_k,
              rwkv_ln_w, rwkv_ln_b, w_out_rwkv,
              s5_a_re, s5_a_im, s5_log_dt, s5_b_re, s5_b_im, s5_c_re, s5_c_im, s5_d, s5_w_glu, w_out_s5,
              m_conv_w, m_conv_b, m_dt_bias, m_a_log, m_d, m_norm, w_out_mamba,
              xa_wq, xa_wk, xa_wv, xa_wo, mlp_w1, mlp_w2):
    f32 = jnp.float32

    def mixer_block(l, xn, rwkv_s, rwkv_shift, s5_re, s5_im, conv_buf, ssm_h):
        proj = xn @ w_in[l]
        gates, p_rwkv, u_s5, z_m, xbc_m, dt_m = split_cols(proj, IN_SIZES)
        gate_r, gate_s, gate_m = split_cols(jax.nn.sigmoid(gates), (D_MODEL, D_MODEL, D_MODEL))
        o_r, rwkv_shift_new, rwkv_s_new = rwkv7_branch(
            p_rwkv, rwkv_shift, rwkv_s, rwkv_mu[l], rwkv_w0[l], rwkv_w2[l], rwkv_a0[l], rwkv_a2[l],
            rwkv_g2[l], rwkv_k_k[l], rwkv_k_a[l], rwkv_r_k[l], rwkv_ln_w[l], rwkv_ln_b[l], w_out_rwkv[l])
        o_s, s5_re_new, s5_im_new = s5_branch(
            u_s5, s5_re, s5_im, s5_a_re[l], s5_a_im[l], s5_log_dt[l], s5_b_re[l], s5_b_im[l],
            s5_c_re[l], s5_c_im[l], s5_d[l], s5_w_glu[l], w_out_s5[l])
        o_m, conv_new, ssm_new = mamba2_branch(
            z_m, xbc_m, dt_m, conv_buf, ssm_h, m_conv_w[l], m_conv_b[l], m_dt_bias[l], m_a_log[l],
            m_d[l], m_norm[l], w_out_mamba[l])
        merged = gate_r * o_r + gate_s * o_s + gate_m * o_m
        return merged @ w_out[l], [rwkv_s_new, rwkv_shift_new, s5_re_new, s5_im_new, conv_new, ssm_new]

    def layer(l, h, mk, mv, st):
        mix, st_new = mixer_block(l, rmsnorm(h, norm_mix_pre[l]), st[0], st[1], st[2], st[3], st[4], st[5])
        h = h + rmsnorm(mix, norm_mix_post[l])
        xa = cross_attend(rmsnorm(h, norm_xa_pre[l]), mk, mv, xa_wq[l], xa_wo[l])
        h = h + rmsnorm(xa, norm_xa_post[l])
        ff = jnp.square(jax.nn.relu(rmsnorm(h, norm_mlp_pre[l]) @ mlp_w1[l])) @ mlp_w2[l]
        h = h + rmsnorm(ff, norm_mlp_post[l])
        return h, st_new

    bp = x_prompt.shape[0]
    zero_states = [jnp.zeros((bp, R_HEADS, R_HEAD, R_HEAD), f32), jnp.zeros((bp, R_COLS), f32),
                   jnp.zeros((bp, S5_GROUPS, S5_STATE), f32), jnp.zeros((bp, S5_GROUPS, S5_STATE), f32),
                   jnp.zeros((bp, M_CONV - 1, M_CONV_DIM), f32), jnp.zeros((bp, M_HEADS, M_HEAD, M_STATE), f32)]
    sample_states = [state_rwkv, state_rwkv_shift, state_s5_re, state_s5_im, state_conv, state_ssm]

    hp, hs = x_prompt, x_sample
    mk_out, mv_out = [], []
    st_p_out = [[] for _ in range(6)]
    st_s_out = [[] for _ in range(6)]
    for l in range(DEPTH):
        mem_n = rmsnorm(mem_prompt, norm_mem[l])
        mk = (mem_n @ xa_wk[l]).reshape(bp, mem_prompt.shape[1], XA_HEADS, XA_HEAD_DIM)
        mv = (mem_n @ xa_wv[l]).reshape(bp, mem_prompt.shape[1], XA_HEADS, XA_HEAD_DIM)
        hp, st_p = layer(l, hp, mk, mv, zero_states)
        hs, st_s = layer(l, hs, cache_mem_k[l], cache_mem_v[l], [s[l] for s in sample_states])
        mk_out.append(mk)
        mv_out.append(mv)
        for i in range(6):
            st_p_out[i].append(st_p[i])
            st_s_out[i].append(st_s[i])

    def stk(xs):
        return jnp.stack(xs).astype(f32)

    return (hp.astype(x_prompt.dtype), hs.astype(x_sample.dtype),
            stk(mk_out), stk(mv_out),
            stk(st_p_out[0]), stk(st_p_out[1]), stk(st_p_out[2]), stk(st_p_out[3]), stk(st_p_out[4]), stk(st_p_out[5]),
            stk(st_s_out[0]), stk(st_s_out[1]), stk(st_s_out[2]), stk(st_s_out[3]), stk(st_s_out[4]), stk(st_s_out[5]))


_drawn_inputs = setup_inputs


def setup_inputs(seed=0):
    import zlib

    import numpy as np

    out = dict(_drawn_inputs(seed))
    spreads = {}
    factors = {'rwkv_w2': 2.848,
     'rwkv_ln_w': 3.609,
     'rwkv_ln_b': 30.855,
     'm_conv_b': 3.127,
     'm_norm': 3.304}
    for name, (base, spread) in spreads.items():
        noise = np.random.default_rng([zlib.crc32(name.encode()), seed]).standard_normal(out[name].shape)
        drawn = base * np.exp(spread * noise) if base else spread * noise
        out[name] = __import__('jax').numpy.asarray(drawn.astype(out[name].dtype))
    for name, factor in factors.items():
        out[name] = (out[name] * factor).astype(out[name].dtype)
    return out
```

```python
from contextlib import ExitStack

import concourse.bass as bass
from concourse import mybir

F32 = mybir.dt.float32
F32R = mybir.dt.float32r
I32 = mybir.dt.int32
ACT = mybir.ActivationFunctionType
ALU = mybir.AluOpType
AX = mybir.AxisListType

P = 128
D = 1024
KD = D // P
SEQ = 1024
NB = 8
TS = 4
NS = NB * TS
NT = SEQ + NS
TC = NT // 3
EPS = 1e-6
R_COLS = 3 * D + 64 + 64 + 128
RT = R_COLS // P
MW = 2 * D
MZ = MW // P
XBC = MW + 1024
MX = XBC // P
C_R = 3 * D
C_S = C_R + R_COLS
C_Z = C_S + D
C_X = C_Z + MW
C_DT = C_X + XBC
ROWS = R_COLS + MW + XBC
TAIL = 3 + NS
RING = 4096
HALF = RING // 2


class Kernel:
    pass


def release(k):
    k.nc.clear_and_free_semaphores(k.sems)
    k.nc.all_engine_barrier()
    k.sems.clear()


def paced(eng, n, unroll, body):
    whole = n // unroll
    if whole > 2:
        with eng.Fori(0, whole) as i:
            for s in range(unroll):
                body(i * unroll + s, s, i)
    else:
        for j in range(whole * unroll):
            body(j, j % unroll, j // unroll)
    for j in range(whole * unroll, n):
        body(j, j % unroll, j // unroll)


def chunks3(t0=0, n=NT):
    out = []
    while n > 0:
        m = min(TC, n)
        out.append((t0, m))
        t0, n = t0 + m, n - m
    return out


class Hooks:
    on = "dve"

    def start(self, eng):
        pass

    def before(self, eng, b, s, r):
        pass

    def after(self, eng, b, s, r):
        pass

    def end(self, eng):
        pass

class Part:

    def __init__(self, W, pair, KT, panels, hooks, pc=None, raw=None, fetch=None):
        self.W, self.pair, self.KT, self.panels, self.hooks, self.raw = W, pair, KT, panels, hooks, raw
        self.pc = pc or HALF // KT
        self.nb = self.pc // P
        self.fetch = fetch
        assert panels % 2 == 0 and (self.nb == 1 or self.nb % 2 == 0)

    def block(self, n, s, r, b):
        return (n, s, r) if self.nb == 1 else (n * self.nb + b, b % 2, n * (self.nb // 2) + b // 2)


def gemm(k, tag, parts, toks):
    nc = k.nc
    nch = len(toks)
    sets = 2
    loaded = [k.sem(f"{tag}_loaded{s}") for s in range(2)]
    w_hi, w_split, panel_used = k.sem(f"{tag}_w_hi"), k.sem(f"{tag}_w_split"), k.sem(f"{tag}_panel_used")
    x_hi, x_split = k.sem(f"{tag}_x_hi"), k.sem(f"{tag}_x_split")
    product = [k.sem(f"{tag}_product{i}") for i in range(len(parts))]
    bank_free = [k.sem(f"{tag}_bank_free{i}") for i in range(len(parts))]
    fetched = [k.sem(f"{tag}_fetched{i}") if p.fetch is not None else None for i, p in enumerate(parts)]
    base = [sum(p.panels for p in parts[:i]) for i in range(len(parts))]
    splits = [sum(p.raw is not None for p in parts[:i + 1]) for i in range(len(parts))]
    with ExitStack() as ctx:
        wh, wl = [ctx.enter_context(nc.sbuf_tensor(f"{tag}_w{x}", [P, 2, HALF], F32R)) for x in ("h", "l")]
        block = ctx.enter_context(nc.Block())

        raw = k.ring[:, 0, :].rearrange("p (s n) -> p s n", s=2)

        def slot(w, p, s):
            return w[:, s, 0:p.KT * p.pc].rearrange("p (t n) -> p t n", t=p.KT)

        def done(i):
            q = parts[i]
            return q.panels * q.nb * nch + sets * nch + 1

        @block.sync
        def _(sp):
            for i, p in enumerate(parts):
                Wv = p.W.rearrange("(t p) n -> p t n", p=P)

                def load(n, s, r):
                    sp.wait_ge(w_split, n + (base[i] + 1))
                    sp.dma_start(slot(raw, p, s), Wv[:, :, bass.ds(n * p.pc, p.pc)]).then_inc(loaded[s], 16)
                paced(sp, p.panels, 2, load)

        @block.tensor
        def _(pe):
            for i, p in enumerate(parts):
                if i:
                    pe.wait_ge(bank_free[i - 1], done(i - 1))

                def panel(n, s, r):
                    pe.wait_ge(w_split, n + (base[i] + 3))
                    for b in range(p.nb):
                        blk, sl, _ = p.block(n, s, r, b)
                        for c, (t0, m) in enumerate(toks):
                            if splits[i]:
                                pe.wait_ge(x_split, (splits[i] - 1) * nch + c + 1)
                            pe.wait_ge(bank_free[i], blk * nch + (c + 1))
                            ps = k.bank[sl * nch + c]
                            for q in range(p.KT):
                                for j, (w, x) in enumerate(((wh, 0), (wh, 1), (wl, 0))):
                                    last = nc.tensor.matmul(ps[:, 0:m], slot(w, p, s)[:, q, b * P:(b + 1) * P], p.pair[x][:, q, t0:t0 + m],
                                                            start=q == 0 and j == 0, stop=q == p.KT - 1 and j == 2)
                            last.then_inc(product[i], 1)
                    pe.drain().then_inc(panel_used, 1)
                paced(pe, p.panels, 2, panel)

        def high(act, i, n, s, r):
            act.wait_ge(loaded[s], 16 * r + (8 * base[i] + 16))
            act.wait_ge(panel_used, n + (base[i] + 1))
            nc.scalar.activation(slot(wh, parts[i], s), slot(raw, parts[i], s), ACT.Copy).then_inc(w_hi, 1)

        def low(dve, i, n, s, r):
            dve.wait_ge(w_hi, n + (base[i] + 1))
            nc.vector.tensor_tensor(slot(wl, parts[i], s), slot(raw, parts[i], s), slot(wh, parts[i], s), ALU.subtract).then_inc(w_split, 1)

        def x_high(act, i):
            p = parts[i]
            if i:
                act.wait_ge(bank_free[i - 1], done(i - 1))
            for t0, m in toks:
                nc.scalar.activation(p.pair[0][:, 0:p.KT, t0:t0 + m], p.raw[:, 0:p.KT, t0:t0 + m], ACT.Copy).then_inc(x_hi, 1)
            if p.fetch is not None:
                act.wait_ge(x_split, splits[i] * nch)
                act.dma_start(p.fetch[0], p.fetch[1]).then_inc(fetched[i], 16)

        def x_low(dve, i):
            p = parts[i]
            for c, (t0, m) in enumerate(toks):
                dve.wait_ge(x_hi, (splits[i] - 1) * nch + c + 1)
                at = (slice(None), slice(0, p.KT), slice(t0, t0 + m))
                nc.vector.tensor_tensor(p.pair[1][at], p.raw[at], p.pair[0][at], ALU.subtract).then_inc(x_split, 1)

        def move_off(eng, name, split, split_x):
            split(eng, 0, 0, 0, 0)
            for i, p in enumerate(parts):
                mine = p.hooks.on == name
                if mine:
                    eng.sem_inc(bank_free[i], sets * nch)
                    p.hooks.start(eng)
                if p.raw is not None:
                    split_x(eng, i)
                if mine and p.fetch is not None:
                    eng.wait_ge(fetched[i], 16)

                def evac(n, s, r):
                    for b in range(p.nb if mine else 0):
                        blk, sl, rnd = p.block(n, s, r, b)
                        p.hooks.before(eng, blk, sl, rnd)
                        for c, (t0, m) in enumerate(toks):
                            eng.wait_ge(product[i], blk * nch + (c + 1))
                            p.hooks.evac(eng, blk, sl, t0, m, k.bank[sl * nch + c]).then_inc(bank_free[i], 1)
                        p.hooks.after(eng, blk, sl, rnd)

                def ahead(n, s, r):
                    split(eng, i, n + 1, 1 - s, r + s)
                    evac(n, s, r)
                rest = p.panels - 2
                paced(eng, rest, 2, ahead)
                ahead(rest, 0, rest // 2)
                if i + 1 < len(parts):
                    split(eng, i + 1, 0, 0, 0)
                evac(rest + 1, 1, rest // 2)
                if mine:
                    p.hooks.end(eng)
                    eng.drain().then_inc(bank_free[i], 1)

        @block.scalar
        def _(act):
            act.sem_inc(panel_used, 2)
            move_off(act, "act", high, x_high)

        @block.vector
        def _(dve):
            dve.sem_inc(w_split, 2)
            move_off(dve, "dve", low, x_low)


class Pair:

    def __init__(self, k, ctx, name, tiles=KD):
        self.parts = [ctx.enter_context(k.nc.sbuf_tensor(f"{name}_{x}", [P, tiles, NT], F32R)) for x in ("hi", "lo")]

    def __getitem__(self, i):
        return self.parts[i]


def norm(k, tag, src, dst, gain, toks, residual=None):
    nc = k.nc
    n = sum(m for _, m in toks)
    squared, summed = k.sem(f"{tag}_squared"), k.sem(f"{tag}_summed")
    rstd_ready, logged = k.sem(f"{tag}_rstd_ready"), k.sem(f"{tag}_logged")
    with ExitStack() as ctx:
        sq = ctx.enter_context(nc.sbuf_tensor(f"{tag}_sq", [P, 2, n], F32))
        rstd = ctx.enter_context(nc.sbuf_tensor(f"{tag}_rstd", [P, n], F32))
        block = ctx.enter_context(nc.Block())

        @block.scalar
        def _(act):
            for q in range(KD):
                if q >= 2:
                    act.wait_ge(summed, q - 1)
                nc.scalar.activation(sq[:, q % 2, :], src[:, q, 0:n], ACT.Square).then_inc(squared, 1)
            act.wait_ge(summed, KD)
            for c, (t0, m) in enumerate(toks):
                nc.scalar.activation(rstd[:, t0:t0 + m], k.bank[c][:, 0:m], ACT.Ln, bias=k.eps[:, 0:1], scale=1.0 / D)
            act.drain()
            nc.scalar.activation(rstd[:, :], rstd[:, :], ACT.Exp, scale=-0.5).then_inc(rstd_ready, 1)

        @block.tensor
        def _(pe):
            for q in range(KD):
                pe.wait_ge(squared, q + 1)
                for c, (t0, m) in enumerate(toks):
                    last = nc.tensor.matmul(k.bank[c][:, 0:m], k.ones[:, :], sq[:, q % 2, t0:t0 + m],
                                            start=q == 0, stop=q == KD - 1)
                last.then_inc(summed, 1)

        @block.vector
        def _(dve):
            dve.wait_ge(rstd_ready, 1)
            for q in range(KD):
                nc.vector.scalar_tensor_tensor(out=dst[:, q, 0:n], in0=src[:, q, 0:n], scalar=gain[:, q:q + 1],
                                               in1=rstd[:, :], op0=ALU.mult, op1=ALU.mult)
            if residual is not None:
                dve.drain()
                for q in range(KD):
                    nc.vector.tensor_tensor(residual[:, q, 0:n], residual[:, q, 0:n], dst[:, q, 0:n], ALU.add)


def constants(k):
    nc = k.nc
    filled, made, rows_in, turned = k.sem("ones_filled"), k.sem("const_made"), k.sem("vec_rows_in"), k.sem("vec_turned")
    with ExitStack() as ctx:
        rows = ctx.enter_context(nc.sbuf_tensor("vec_rows", [P, 3, P], F32))
        block = ctx.enter_context(nc.Block())

        @block.gpsimd
        def _(pool):
            pool.wait_ge(filled, 1)
            pool.affine_select(out=k.ident[:, :], in_=k.ones[:, :], compare_op=ALU.is_equal, fill=0.0, base=0,
                               pattern=[[-1, P]], channel_multiplier=1)
            pool.drain()
            pool.affine_select(out=k.upper[:, :], in_=k.ones[:, :], compare_op=ALU.is_ge, fill=0.0, base=0,
                               pattern=[[1, P]], channel_multiplier=-1)
            pool.drain().then_inc(made, 1)

        @block.sync
        def _(sp):
            for name, tile, row, src in k.vec_rows:
                n = src.shape[0]
                sp.dma_start(rows[row:row + n, tile, :], src).then_inc(rows_in, 16)

        @block.tensor
        def _(pe):
            pe.wait_ge(made, 1)
            pe.wait_ge(rows_in, 16 * len(k.vec_rows))
            for tile, used in enumerate(k.vec_used):
                last = nc.tensor.transpose(k.bank[0][:, tile * P:tile * P + used], rows[0:used, tile, :],
                                           k.ident[0:used, 0:used])
            last.then_inc(turned, 1)

        @block.vector
        def _(dve):
            nc.vector.memset(k.ones[:, :], 1.0).then_inc(filled, 1)
            nc.vector.memset(k.ones64[:, :], 0.0)
            nc.vector.memset(k.eps[:, 0:1], EPS)
            nc.vector.memset(k.eps[:, 1:2], 1e-12)
            nc.vector.memset(k.eps[:, 2:3], 64e-5)
            dve.drain()
            nc.vector.memset(k.ones64[0:64, 0:64], 1.0)
            nc.vector.memset(k.ones64[64:128, 64:128], 1.0)
            dve.wait_ge(turned, 1)
            for tile, used in enumerate(k.vec_used):
                nc.vector.tensor_copy(k.vec[:, tile * P:tile * P + used], k.bank[0][:, tile * P:tile * P + used])


def load_tokens(k, tag, src, sample, dst):
    nc = k.nc
    a = src.shape[0] // P
    in_, turned, copied = k.sem(f"{tag}_in"), k.sem(f"{tag}_turned"), k.sem(f"{tag}_copied")
    with ExitStack() as ctx:
        xs = ctx.enter_context(nc.sbuf_tensor(f"{tag}_rows", [P, a, D], F32))
        xm = ctx.enter_context(nc.sbuf_tensor(f"{tag}_sample", [NS, D], F32)) if sample is not None else None
        block = ctx.enter_context(nc.Block())
        steps = [(j, h) for j in range(a) for h in range(KD // 4)]

        @block.sync
        def _(sp):
            for j in range(a):
                sp.dma_start(xs[:, j, :], src[j * P:(j + 1) * P, :]).then_inc(in_, 16)
            if sample is not None:
                sp.dma_start(xm[:, :], sample).then_inc(in_, 16)

        @block.tensor
        def _(pe):
            pe.wait_ge(in_, 16 * (a + (sample is not None)))
            for n, (j, h) in enumerate(steps):
                if n >= 4:
                    pe.wait_ge(copied, n - 3)
                for q in range(4):
                    last = nc.tensor.transpose(k.bank[n % 4][:, q * P:(q + 1) * P],
                                               xs[:, j, (4 * h + q) * P:(4 * h + q + 1) * P], k.ident[:, :])
                last.then_inc(turned, 1)
            if sample is not None:
                for q in range(KD):
                    last = nc.tensor.transpose(k.bank[4][:, q * NS:(q + 1) * NS], xm[:, q * P:(q + 1) * P],
                                               k.ident[0:NS, 0:NS])
                last.then_inc(turned, 1)

        @block.vector
        def _(dve):
            for n, (j, h) in enumerate(steps):
                dve.wait_ge(turned, n + 1)
                nc.vector.tensor_copy(dst[:, 4 * h:4 * h + 4, j * P:(j + 1) * P],
                                      k.bank[n % 4][:, :].rearrange("p (q t) -> p q t", q=4)).then_inc(copied, 1)
            if sample is not None:
                dve.wait_ge(turned, len(steps) + 1)
                nc.vector.tensor_copy(dst[:, :, SEQ:NT],
                                      k.bank[4][:, 0:KD * NS].rearrange("p (q t) -> p q t", q=KD))


class StoreRows(Hooks):
    on = "act"

    def __init__(self, k, tag, dst, staging, func=ACT.Copy):
        self.k, self.staging, self.func = k, staging, func
        self.dst, self.blocks = dst.rearrange("(b p) t -> p b t", p=P), dst.shape[0] // P
        self.stored = [k.sem(f"{tag}_stored{s}") for s in range(2)]

    def start(self, act):
        for stored in self.stored:
            act.sem_inc(stored, 16)

    def before(self, act, b, s, r):
        act.wait_ge(self.stored[s], 16 * r + 16)

    def evac(self, act, b, s, t0, m, ps):
        return self.k.nc.scalar.activation(self.staging[:, s, t0:t0 + m], ps[:, 0:m], self.func)

    def after(self, act, b, s, r):
        act.drain()
        act.dma_start(self.dst[:, bass.ds(b, 1), :], self.staging[:, s:s + 1, :]).then_inc(self.stored[s], 16)

    def end(self, act):
        for stored in self.stored:
            act.wait_ge(stored, 8 * self.blocks + 16)


def project_to_dram(k, xnT):
    nc = k.nc
    with nc.sbuf_tensor("proj_staging", [P, 2, NT], F32) as staging, ExitStack() as ctx:
        pair, parts = Pair(k, ctx, "xn"), []
        for tag, col, dst, pc, func in (("pg", 0, k.gates, 256, ACT.Sigmoid),
                                        ("pr", C_R, k.proj[0:3 * D, :], 256, ACT.Copy),
                                        ("pl", C_R + 3 * D, k.proj[3 * D:R_COLS, :], 128, ACT.Copy),
                                        ("pz", C_Z, k.proj[R_COLS:ROWS, :], 256, ACT.Copy)):
            n = dst.shape[0]
            parts.append(Part(k.w_in[:, col:col + n], pair, KD, n // pc, StoreRows(k, tag, dst, staging, func), pc,
                              raw=None if parts else xnT))
        gemm(k, "proj", parts, chunks3())
    wdt_in, product = k.sem("wdt_in"), k.sem("dt_product")
    with ExitStack() as ctx:
        wdt = ctx.enter_context(nc.sbuf_tensor("wdt", [P, KD, 32], F32))
        block = ctx.enter_context(nc.Block())

        @block.sync
        def _(sp):
            sp.dma_start(wdt[:, :, :], k.w_in[:, C_DT:C_DT + 32].rearrange("(t p) n -> p t n", p=P)).then_inc(wdt_in, 16)

        @block.tensor
        def _(pe):
            pe.wait_ge(wdt_in, 16)
            for c, (t0, m) in enumerate(chunks3()):
                for q in range(KD):
                    last = nc.tensor.matmul(k.bank[c][0:32, 0:m], wdt[:, q, :], xnT[:, q, t0:t0 + m],
                                            start=q == 0, stop=q == KD - 1)
                last.then_inc(product, 1)

        @block.vector
        def _(dve):
            for c, (t0, m) in enumerate(chunks3()):
                dve.wait_ge(product, c + 1)
                nc.vector.tensor_copy(k.dtT[:, t0:t0 + m], k.bank[c][0:32, 0:m])


def tails(k, tailT):
    nc = k.nc
    tiles = ROWS // P
    groups = [(g, min(4, tiles - 4 * g)) for g in range((tiles + 3) // 4)]
    in_, turned, copied, out = k.sem("tail_in"), k.sem("tail_turned"), k.sem("tail_copied"), k.sem("tail_out")
    with ExitStack() as ctx:
        rows = ctx.enter_context(nc.sbuf_tensor("tail_rows", [TAIL, ROWS], F32))
        block = ctx.enter_context(nc.Block())

        @block.sync
        def _(sp):
            sp.dma_start(tailT[:, :, :], k.proj[:, SEQ - 3:NT].rearrange("(b p) t -> p b t", p=P)).then_inc(in_, 16)
            sp.wait_ge(copied, len(groups))
            o = k.out
            sp.dma_start(o["rwkv_shift_prompt"][0, :, :], rows[2:3, 0:R_COLS]).then_inc(out, 16)
            sp.dma_start(o["rwkv_shift_sample"][0, :, :], rows[3 + TS - 1:TAIL:TS, 0:R_COLS]).then_inc(out, 16)
            x0 = R_COLS + MW
            sp.dma_start(o["conv_prompt"][0, 0, :, :], rows[0:3, x0:ROWS]).then_inc(out, 16)
            for b in range(NB):
                first = 3 + TS * b + 1
                sp.dma_start(o["conv_sample"][0, b, :, :], rows[first:first + 3, x0:ROWS]).then_inc(out, 16)
            sp.wait_ge(out, 16 * (3 + NB))

        @block.tensor
        def _(pe):
            pe.wait_ge(in_, 16)
            for g, n in groups:
                if g >= 4:
                    pe.wait_ge(copied, g - 3)
                for q in range(n):
                    last = nc.tensor.transpose(k.bank[g % 4][0:TAIL, q * P:(q + 1) * P], tailT[:, 4 * g + q, :], k.ident[:, :])
                last.then_inc(turned, 1)

        @block.vector
        def _(dve):
            for g, n in groups:
                dve.wait_ge(turned, g + 1)
                nc.vector.tensor_copy(rows[:, 4 * g * P:(4 * g + n) * P], k.bank[g % 4][0:TAIL, 0:n * P]).then_inc(copied, 1)


class Keep(Hooks):
    on = "act"

    def __init__(self, k, dst, func=ACT.Copy):
        self.k, self.dst, self.func = k, dst, func

    def evac(self, act, b, s, t0, m, ps):
        return self.k.nc.scalar.activation(self.dst[:, bass.ds(b, 1), t0:t0 + m], ps[:, 0:m], self.func)


class Gate(Hooks):

    def __init__(self, k, g, merged):
        self.k, self.g, self.merged = k, g, merged

    def evac(self, dve, b, s, t0, m, ps):
        at = self.g[:, bass.ds(b, 1), t0:t0 + m]
        return self.k.nc.vector.tensor_tensor(at, ps[:, 0:m].unsqueeze(1), at, ALU.mult)

    def after(self, dve, b, s, r):
        dve.drain()
        at = (slice(None), bass.ds(b, 1), slice(None))
        self.k.nc.vector.tensor_tensor(self.merged[at], self.merged[at], self.g[at], ALU.add)


class Accumulate(Hooks):

    def __init__(self, k, dst, first, g=None):
        self.k, self.dst, self.first, self.g = k, dst, first, g

    def evac(self, dve, b, s, t0, m, ps):
        d = self.dst[:, b, t0:t0 + m]
        if self.first:
            return self.k.nc.vector.tensor_copy(d, ps[:, 0:m])
        return self.k.nc.vector.tensor_tensor(d, ps[:, 0:m], d, ALU.add)

    def after(self, dve, b, s, r):
        if self.g is not None:
            dve.drain()
            self.k.nc.vector.tensor_tensor(self.dst[:, b, :], self.dst[:, b, :], self.g[:, b, :], ALU.mult)


class Squares(Hooks):

    def __init__(self, k, pair, t):
        self.k, self.pair, self.t = k, pair, t

    def evac(self, dve, b, s, t0, m, ps):
        return self.k.nc.vector.tensor_scalar(self.t[:, s, t0:t0 + m], ps[:, 0:m], 0.0, None, ALU.max)

    def after(self, dve, b, s, r):
        nc, t = self.k.nc, self.t[:, s, :]
        dve.drain()
        nc.vector.tensor_tensor(t, t, t, ALU.mult)
        dve.drain()
        nc.vector.tensor_copy(self.pair[0][:, b, :], t)
        dve.drain()
        nc.vector.tensor_tensor(self.pair[1][:, b, :], t, self.pair[0][:, b, :], ALU.subtract)


def product(k, tag, W, x, dst, func=ACT.Copy):
    with ExitStack() as ctx:
        gemm(k, tag, [Part(W, Pair(k, ctx, f"{tag}_x"), KD, 4, Keep(k, dst, func), raw=x)], chunks3())


def mlp(k, xn, out):
    w1, w2 = k.w["mlp_w1"][0], k.w["mlp_w2"][0]
    EIGHTH = w1.shape[1] // 8
    with ExitStack() as ctx:
        x, hidden = Pair(k, ctx, "mlp_x"), Pair(k, ctx, "mlp_hidden", EIGHTH // P)
        t = k.ring[:, 1, 0:2 * NT].rearrange("p (s t) -> p s t", s=2)
        parts = []
        for q in range(8):
            at = slice(q * EIGHTH, (q + 1) * EIGHTH)
            parts.append(Part(w1[:, at], x, KD, 2, Squares(k, hidden, t), raw=xn if q == 0 else None))
            parts.append(Part(w2[at, :], hidden, EIGHTH // P, 2, Accumulate(k, out, q == 0)))
        gemm(k, "mlp", parts, chunks3())


def store_tokens(k, hT):
    nc = k.nc
    turned, copied, stored = k.sem("y_turned"), k.sem("y_copied"), [k.sem(f"y_stored{s}") for s in range(2)]
    y, ys = k.out["y_prompt"][0], k.out["y_sample"].rearrange("b t d -> (b t) d")
    tiles = SEQ // P + 1
    with ExitStack() as ctx:
        rows = ctx.enter_context(nc.sbuf_tensor("y_rows", [P, 2, D], F32))
        block = ctx.enter_context(nc.Block())

        def size(j):
            return P if j < SEQ // P else NS

        @block.tensor
        def _(pe):
            for j in range(tiles):
                for h in range(2):
                    n = 2 * j + h
                    if n >= 4:
                        pe.wait_ge(copied, n - 3)
                    for q in range(4):
                        last = nc.tensor.transpose(k.bank[n % 4][0:size(j), q * P:(q + 1) * P],
                                                   hT[:, 4 * h + q, j * P:j * P + size(j)], k.ident[:, :])
                    last.then_inc(turned, 1)

        @block.vector
        def _(dve):
            for j in range(tiles):
                if j >= 2:
                    dve.wait_ge(stored[j % 2], 16 * (j // 2))
                for h in range(2):
                    n = 2 * j + h
                    dve.wait_ge(turned, n + 1)
                    nc.vector.tensor_copy(rows[0:size(j), j % 2, 512 * h:512 * (h + 1)], k.bank[n % 4][0:size(j), :]).then_inc(copied, 1)

        @block.sync
        def _(sp):
            for j in range(tiles):
                sp.wait_ge(copied, 2 * j + 2)
                dst = y[j * P:(j + 1) * P, :] if j < SEQ // P else ys
                sp.dma_start(dst, rows[0:size(j), j % 2, :]).then_inc(stored[j % 2], 16)
            for s in range(2):
                sp.wait_ge(stored[s], 16 * ((tiles + 1 - s) // 2))


def gemm_rows(k, tag, W, lhs, evac):
    nc = k.nc
    loaded, product, off = [k.sem(f"{tag}_loaded{s}") for s in range(2)], k.sem(f"{tag}_product"), k.sem(f"{tag}_off")
    with nc.Block() as block:
        @block.sync
        def _(sp):
            for s in range(2):
                sp.dma_start(k.ring[:, s, :].rearrange("p (t n) -> p t n", t=KD),
                             W[:, s * 512:(s + 1) * 512].rearrange("(t p) n -> p t n", p=P)).then_inc(loaded[s], 16)

        @block.tensor
        def _(pe):
            n = 0
            for s in range(2):
                pe.wait_ge(loaded[s], 16)
                w = k.ring[:, s, :].rearrange("p (t n) -> p t n", t=KD)
                for x, rows in lhs:
                    if n >= 4:
                        pe.wait_ge(off, n - 3)
                    for q in range(KD):
                        last = nc.tensor.matmul(k.bank[n % 4][0:rows, :], x(q), w[:, q, :], start=q == 0, stop=q == KD - 1)
                    last.then_inc(product, 1)
                    n += 1

        @block.vector
        def _(dve):
            n = 0
            for s in range(2):
                for i, (x, rows) in enumerate(lhs):
                    dve.wait_ge(product, n + 1)
                    evac(dve, i, s, k.bank[n % 4][0:rows, :]).then_inc(off, 1)
                    n += 1


def attend_prompt(k, qT, oT, keyT, val):
    nc = k.nc
    scale = 256 ** -0.5
    units = [(h, t) for h in range(4) for t in range(2)]
    scored, peaked, probed, scaled = k.sem("xp_scored"), k.sem("xp_peaked"), k.sem("xp_probed"), k.sem("xp_scaled")
    turned, turned_off, mixed, mixed_off = k.sem("xp_turned"), k.sem("xp_turned_off"), k.sem("xp_mixed"), k.sem("xp_mixed_off")
    with ExitStack() as ctx:
        pr = ctx.enter_context(nc.sbuf_tensor("xp_probs", [P, 2, 4, 256], F32))
        pT = ctx.enter_context(nc.sbuf_tensor("xp_probsT", [P, 2, 2, 512], F32))
        st = ctx.enter_context(nc.sbuf_tensor("xp_stats", [P, 2, 3, 4], F32))
        block = ctx.enter_context(nc.Block())

        @block.tensor
        def _(pe):
            def scores(n):
                h, t = units[n]
                if n >= 1:
                    pe.wait_ge(probed, n)
                for i in range(4):
                    for d in range(2):
                        last = nc.tensor.matmul(k.bank[i // 2][:, (i % 2) * 256:(i % 2) * 256 + 256],
                                                qT[:, 2 * h + d, t * 512 + i * P:t * 512 + (i + 1) * P],
                                                keyT[:, 2 * h + d, :], start=d == 0, stop=d == 1)
                last.then_inc(scored, 1)

            scores(0)
            for n, (h, t) in enumerate(units):
                pe.wait_ge(scaled, n + 1)
                if n + 1 < len(units):
                    scores(n + 1)
                if n >= 1:
                    pe.wait_ge(turned_off, n)
                for mt in range(2):
                    for i in range(4):
                        last = nc.tensor.transpose(k.bank[2 + mt][:, i * P:(i + 1) * P], pr[:, n % 2, i, mt * P:(mt + 1) * P], k.ident[:, :])
                last.then_inc(turned, 1)
                pe.wait_ge(turned_off, n + 1)
                if n >= 1:
                    pe.wait_ge(mixed_off, n)
                for d in range(2):
                    for mt in range(2):
                        last = nc.tensor.matmul(k.bank[4 + d][:, :], val[:, mt, (2 * h + d) * P:(2 * h + d + 1) * P],
                                                pT[:, n % 2, mt, :], start=mt == 0, stop=mt == 1)
                last.then_inc(mixed, 1)

        @block.vector
        def _(dve):
            for n, (h, t) in enumerate(units):
                s = st[:, n % 2]
                dve.wait_ge(scored, n + 1)
                for i in range(2):
                    nc.vector.reduce_max(s[:, 0, 2 * i:2 * i + 2], k.bank[i][:, :].rearrange("p (a m) -> p a m", a=2), AX.X)
                dve.drain()
                nc.vector.tensor_scalar(s[:, 0, :], s[:, 0, :], -scale, None, ALU.mult).then_inc(peaked, 1)
                dve.wait_ge(probed, n + 1)
                nc.vector.reciprocal(s[:, 2, :], s[:, 1, :])
                dve.drain()
                for i in range(4):
                    last = nc.vector.tensor_scalar(pr[:, n % 2, i, :], pr[:, n % 2, i, :], s[:, 2, i:i + 1], None, ALU.mult)
                last.then_inc(scaled, 1)
                dve.wait_ge(turned, n + 1)
                for mt in range(2):
                    last = nc.vector.tensor_copy(pT[:, n % 2, mt, :], k.bank[2 + mt][:, :])
                last.then_inc(turned_off, 1)

        @block.scalar
        def _(act):
            for n, (h, t) in enumerate(units):
                s = st[:, n % 2]
                act.wait_ge(peaked, n + 1)
                for i in range(4):
                    last = nc.scalar.activation(pr[:, n % 2, i, :], k.bank[i // 2][:, (i % 2) * 256:(i % 2) * 256 + 256], ACT.Exp,
                                                bias=s[:, 0, i:i + 1], scale=scale, accum_out=s[:, 1, i:i + 1])
                last.then_inc(probed, 1)
                act.wait_ge(mixed, n + 1)
                for d in range(2):
                    last = nc.scalar.activation(oT[:, 2 * h + d, t * 512:(t + 1) * 512], k.bank[4 + d][:, :], ACT.Copy)
                last.then_inc(mixed_off, 1)


def attend_samples(k, qT, oT):
    nc = k.nc
    scale = 256 ** -0.5
    ck, cv = k.w["cache_mem_k"][0].rearrange("b m h d -> b m (h d)"), k.w["cache_mem_v"][0].rearrange("b m h d -> b m (h d)")
    k_in, v_in = [k.sem(f"xs_k_in{s}") for s in range(2)], [k.sem(f"xs_v_in{s}") for s in range(2)]
    turned, turned_off, spread, scored, k_used = (k.sem("xs_turned"), k.sem("xs_turned_off"), k.sem("xs_spread"),
                                                  k.sem("xs_scored"), k.sem("xs_k_used"))
    peaked, probed, scaled, p_turned, p_off = (k.sem("xs_peaked"), k.sem("xs_probed"), k.sem("xs_scaled"),
                                               k.sem("xs_p_turned"), k.sem("xs_p_off"))
    mixed = k.sem("xs_mixed")
    with ExitStack() as ctx:
        def sb(name, shape):
            return ctx.enter_context(nc.sbuf_tensor(name, shape, F32))
        kb, vb = [k.ring[:, i, :].rearrange("p (s a c) -> p s a c", s=2, a=2) for i in range(2)]
        kT = sb("xs_kT", [P, 2, KD, 256])
        qz = sb("xs_q", [P, KD, NB * 36])
        pr, pT, st = sb("xs_probs", [NS, 4, 256]), sb("xs_probsT", [P, 8, NS]), sb("xs_stats", [NS, 3, 4])
        block = ctx.enter_context(nc.Block())

        @block.sync
        def _(sp):
            for b in range(NB):
                if b >= 2:
                    sp.wait_ge(k_used, b - 1)
                sp.dma_start(kb[:, b % 2, :, :], ck[b].rearrange("(a p) c -> p a c", p=P)).then_inc(k_in[b % 2], 16)
            for b in range(NB):
                if b >= 2:
                    sp.wait_ge(mixed, b - 1)
                sp.dma_start(vb[:, b % 2, :, :], cv[b].rearrange("(a p) c -> p a c", p=P)).then_inc(v_in[b % 2], 16)

        @block.tensor
        def _(pe):
            pe.wait_ge(spread, 1)
            for b in range(NB):
                pe.wait_ge(k_in[b % 2], 16 * (b // 2 + 1))
                for g in range(4):
                    n = 4 * b + g
                    if n >= 4:
                        pe.wait_ge(turned_off, n - 3)
                    for d in range(2):
                        for a in range(2):
                            last = nc.tensor.transpose(k.bank[4 + g][:, (2 * d + a) * P:(2 * d + a + 1) * P],
                                                       kb[:, b % 2, a, (2 * g + d) * P:(2 * g + d + 1) * P], k.ident[:, :])
                    last.then_inc(turned, 1)
                pe.drain().then_inc(k_used, 1)
                pe.wait_ge(turned_off, 4 * b + 4)
                for h in range(4):
                    for d in range(2):
                        last = nc.tensor.matmul(k.bank[h][0:NS, 0:256], qz[:, 2 * h + d, 32 * b:32 * b + 32], kT[:, b % 2, 2 * h + d, :],
                                                start=b == 0 and d == 0, stop=b == NB - 1 and d == 1)
                last.then_inc(scored, 1)
            pe.wait_ge(scaled, 1)
            for h in range(4):
                for a in range(2):
                    last = nc.tensor.transpose(k.bank[4][:, (2 * h + a) * NS:(2 * h + a + 1) * NS], pr[:, h, a * P:(a + 1) * P],
                                               k.ident[0:NS, 0:NS])
            last.then_inc(p_turned, 1)
            pe.wait_ge(p_off, 1)
            for b in range(NB):
                pe.wait_ge(v_in[b % 2], 16 * (b // 2 + 1))
                for f in range(KD):
                    for a in range(2):
                        last = nc.tensor.matmul(k.bank[5][:, f * NS + TS * b:f * NS + TS * b + TS], vb[:, b % 2, a, f * P:(f + 1) * P],
                                                pT[:, 2 * (f // 2) + a, TS * b:TS * b + TS], start=a == 0, stop=a == 1)
                last.then_inc(mixed, 1)

        @block.vector
        def _(dve):
            nc.vector.memset(qz[:, :, :], 0.0)
            dve.drain()
            nc.vector.tensor_copy(qz[:, :, :].rearrange("p f (b r) -> p f b r", r=36)[:, :, :, 0:TS],
                                  qT[:, :, SEQ:NT].rearrange("p f (b t) -> p f b t", t=TS)).then_inc(spread, 1)
            for n in range(4 * NB):
                b, g = n // 4, n % 4
                dve.wait_ge(turned, n + 1)
                if b >= 2:
                    dve.wait_ge(scored, b - 1)
                nc.vector.tensor_copy(kT[:, b % 2, 2 * g:2 * g + 2, :],
                                      k.bank[4 + g][:, :].rearrange("p (f m) -> p f m", f=2)).then_inc(turned_off, 1)
            dve.wait_ge(scored, NB)
            for h in range(4):
                nc.vector.reduce_max(st[:, 0, h:h + 1], k.bank[h][0:NS, 0:256], AX.X)
            dve.drain()
            nc.vector.tensor_scalar(st[:, 0, :], st[:, 0, :], -scale, None, ALU.mult).then_inc(peaked, 1)
            dve.wait_ge(probed, 1)
            nc.vector.reciprocal(st[:, 2, :], st[:, 1, :])
            dve.drain()
            for h in range(4):
                last = nc.vector.tensor_scalar(pr[:, h, :], pr[:, h, :], st[:, 2, h:h + 1], None, ALU.mult)
            last.then_inc(scaled, 1)
            dve.wait_ge(p_turned, 1)
            nc.vector.tensor_copy(pT[:, :, :], k.bank[4][:, 0:8 * NS].rearrange("p (a t) -> p a t", t=NS)).then_inc(p_off, 1)
            dve.wait_ge(mixed, NB)
            nc.vector.tensor_copy(oT[:, :, SEQ:NT], k.bank[5][:, 0:KD * NS].rearrange("p (f t) -> p f t", f=KD))

        @block.scalar
        def _(act):
            act.wait_ge(peaked, 1)
            for h in range(4):
                last = nc.scalar.activation(pr[:, h, :], k.bank[h][0:NS, 0:256], ACT.Exp, bias=st[:, 0, h:h + 1], scale=scale,
                                            accum_out=st[:, 1, h:h + 1])
            last.then_inc(probed, 1)


def memory(k, keyT, val):
    nc = k.nc
    M = 256
    with nc.sbuf_tensor("memT", [P, KD, M], F32) as memT, nc.sbuf_tensor("key_rows", [P, 2, D], F32) as key:
        load_tokens(k, "mem", k.w["mem_prompt"][0], None, memT)
        norm(k, "memn", memT, memT, k.col["norm_mem"], [(0, M)])
        for tag, W, dst, out in (("memk", k.w["xa_wk"][0], key, k.out["mem_k_prompt"]), ("memv", k.w["xa_wv"][0], val, k.out["mem_v_prompt"])):
            lhs = [((lambda q, a=a: memT[:, q, a * P:(a + 1) * P]), P) for a in range(2)]
            gemm_rows(k, tag, W, lhs, lambda dve, i, s, ps, dst=dst: nc.vector.tensor_copy(dst[:, i, s * 512:(s + 1) * 512], ps))
        out, turned, off = k.sem("mem_out"), k.sem("memk_turned"), k.sem("memk_turned_off")
        with nc.Block() as block:
            @block.sync
            def _(sp):
                for src, o in ((key, "mem_k_prompt"), (val, "mem_v_prompt")):
                    sp.dma_start(k.out[o][0, 0].rearrange("(a p) h d -> p a (h d)", p=P), src[:, :, :]).then_inc(out, 16)
                sp.wait_ge(out, 32)

            @block.tensor
            def _(pe):
                for g in range(4):
                    for d in range(2):
                        for a in range(2):
                            last = nc.tensor.transpose(k.bank[g][:, (2 * d + a) * P:(2 * d + a + 1) * P],
                                                       key[:, a, (2 * g + d) * P:(2 * g + d + 1) * P], k.ident[:, :])
                    last.then_inc(turned, 1)

            @block.vector
            def _(dve):
                for g in range(4):
                    dve.wait_ge(turned, g + 1)
                    nc.vector.tensor_copy(keyT[:, 2 * g:2 * g + 2, :], k.bank[g][:, :].rearrange("p (f m) -> p f m", f=2))


def move(k, tag, dst, src):
    done = k.sem(f"{tag}_moved")
    with k.nc.Block() as block:
        @block.sync
        def _(sp):
            sp.dma_start(dst, src).then_inc(done, 16)
            sp.wait_ge(done, 16)


def attention(k, both):
    nc = k.nc
    hT, xT = both[:, 0:KD, :], both[:, KD:2 * KD, :]
    norm(k, "xapre", hT, xT, k.col["norm_xa_pre"], chunks3())
    product(k, "xq", k.w["xa_wq"][0], xT, xT)
    with nc.sbuf_tensor("keyT", [P, KD, 256], F32) as keyT, nc.sbuf_tensor("val", [P, 2, D], F32) as val:
        memory(k, keyT, val)
        attend_prompt(k, xT, xT, keyT, val)
        attend_samples(k, xT, xT)
    product(k, "xo", k.w["xa_wo"][0], xT, xT)
    norm(k, "xapost", xT, xT, k.col["norm_xa_post"], chunks3(), residual=hT)
    norm(k, "mlppre", hT, xT, k.col["norm_mlp_pre"], chunks3())
    move(k, "h_off", k.h_dram, hT)
    move(k, "mlp_in", k.xn_dram, xT)


def mlp_sublayer(k):
    nc = k.nc
    with nc.sbuf_tensor("mlp_io", [P, KD, NT], F32) as x:
        move(k, "mlp_xn", x[:, :, :], k.xn_dram)
        mlp(k, x, x)
        with nc.sbuf_tensor("mlp_h", [P, KD, NT], F32) as h:
            move(k, "h_on", h[:, :, :], k.h_dram)
            norm(k, "mlppost", x, x, k.col["norm_mlp_post"], chunks3(), residual=h)
            store_tokens(k, h)


def exact_exp(dve, nc, x, n, r, p, bits):
    def op(f, *a, **kw):
        f(*a, **kw)
        dve.drain()
    ts, tt, stt = nc.vector.tensor_scalar, nc.vector.tensor_tensor, nc.vector.scalar_tensor_tensor
    magic = 12582912.0
    op(ts, n, x, 1.4426950408889634, magic, ALU.mult, ALU.add)
    op(ts, n, n, -magic, None, ALU.add)
    op(ts, n, n, -126.0, 127.0, ALU.max, ALU.min)
    op(ts, r, n, 0.693359375, None, ALU.mult)
    op(tt, r, x, r, ALU.subtract)
    op(ts, p, n, -2.12194440054690583e-4, None, ALU.mult)
    op(tt, r, r, p, ALU.subtract)
    op(ts, p, r, 1.0 / 5040, None, ALU.mult)
    for c in (1.0 / 720, 1.0 / 120, 1.0 / 24, 1.0 / 6, 0.5, 1.0):
        op(stt, out=p, in0=p, scalar=c, in1=r, op0=ALU.add, op1=ALU.mult)
    op(ts, p, p, 1.0, None, ALU.add)
    op(ts, n, n, 127.0, 8388608.0, ALU.add, ALU.mult)
    op(nc.vector.tensor_copy, bits, n)
    op(tt, p, p, bits.bitcast(F32), ALU.mult)


Q5 = 8
PAIRS = 32
QP = 8
GC = 16


def s5_params(k, v):
    nc, w = k.nc, k.w
    rows_in, b_in, c_in, stated = k.sem("s5p_rows_in"), k.sem("s5p_b_in"), k.sem("s5p_c_in"), k.sem("s5p_states_in")
    turned, reduced, sines, spread = k.sem("s5p_turned"), k.sem("s5p_reduced"), k.sem("s5p_sines"), k.sem("s5p_spread")
    with ExitStack() as ctx:
        def sb(name, shape):
            return ctx.enter_context(nc.sbuf_tensor(f"s5p_{name}", shape, F32))
        rows, dtr = sb("rows", [PAIRS, 3, P]), sb("dt_rows", [PAIRS, 2])
        cr = k.ring[:, :, 0:1024].rearrange("p i (a n) -> p i a n", n=P)
        h0r = sb("h0_rows", [P, 2, 2, P])
        braw = sb("b_raw", [P, 2, PAIRS, GC])
        t = sb("tmp", [P, 16, PAIRS])
        tb = sb("tmp_b", [P, PAIRS, GC])
        bits = ctx.enter_context(nc.sbuf_tensor("s5p_bits", [P, PAIRS], I32))
        block = ctx.enter_context(nc.Block())

        @block.sync
        def _(sp):
            for i, n in enumerate(("s5_a_re", "s5_a_im")):
                sp.dma_start(rows[:, i, :], w[n][0].rearrange("(q h) p -> q (h p)", h=2)).then_inc(rows_in, 16)
            sp.dma_start(dtr[:, :], w["s5_log_dt"][0].rearrange("(q h) -> q h", h=2)).then_inc(rows_in, 16)
            for i, n in enumerate(("s5_c_re", "s5_c_im")):
                src = w[n][0].rearrange("(a g) c p -> (g c) a p", g=8)
                for half in range(2):
                    sp.dma_start(cr[:, i, :, 64 * half:64 * half + 64], src).then_inc(c_in, 16)
            for i, n in enumerate(("state_s5_re", "state_s5_im")):
                sp.dma_start(h0r[:, i, :, :], w[n][0].rearrange("(a b) (q h) p -> (b q) a (h p)", a=2, h=2)).then_inc(stated, 16)
            for i, n in enumerate(("s5_b_re", "s5_b_im")):
                src = w[n][0].rearrange("(q h) p c -> h p q c", h=2)
                for half in range(2):
                    sp.dma_start(braw[64 * half:64 * half + 64, i, :, :], src[half]).then_inc(b_in, 16)

        @block.tensor
        def _(pe):
            pe.wait_ge(rows_in, 48)
            pe.wait_ge(spread, 1)
            for i in range(3):
                nc.tensor.transpose(k.bank[0][:, i * 32:(i + 1) * 32], rows[:, i, :], k.ident[0:32, 0:32])
            pe.wait_ge(c_in, 64)
            for i in range(2):
                for a in range(8):
                    nc.tensor.transpose(k.bank[1 + 2 * i + a // 4][:, (a % 4) * P:(a % 4 + 1) * P], cr[:, i, a, :], k.ident[:, :])
            pe.wait_ge(stated, 32)
            for i in range(2):
                for a in range(2):
                    last = nc.tensor.transpose(k.bank[5][:, (2 * i + a) * P:(2 * i + a + 1) * P], h0r[:, i, a, :], k.ident[:, :])
            last.then_inc(turned, 1)

        @block.scalar
        def _(act):
            act.wait_ge(reduced, 1)
            nc.scalar.activation(t[:, 7, :], t[:, 5, :], ACT.Sin)
            nc.scalar.activation(t[:, 8, :], t[:, 6, :], ACT.Sin)
            act.drain().then_inc(sines, 1)

        @block.vector
        def _(dve):
            tt, ts = nc.vector.tensor_tensor, nc.vector.tensor_scalar

            def op(f, *a, **kw):
                f(*a, **kw)
                dve.drain()
            dve.wait_ge(rows_in, 48)
            nc.vector.tensor_copy(rows[:, 2, :].rearrange("q (h p) -> q h p", h=2), dtr[:, :].unsqueeze(2).broadcast_to([PAIRS, 2, 64]))
            dve.drain().then_inc(spread, 1)
            dve.wait_ge(turned, 1)
            op(nc.vector.tensor_copy, t[:, 0:3, :], k.bank[0][:, 0:96].rearrange("p (i q) -> p i q", i=3))
            are, aim, dt = t[:, 0, :], t[:, 1, :], t[:, 2, :]
            op(nc.vector.tensor_copy, t[:, 15, :], dt)
            exact_exp(dve, nc, t[:, 15, :], t[:, 12, :], t[:, 13, :], dt, bits[:, :])
            op(tt, t[:, 15, :], dt, are, ALU.mult)
            exact_exp(dve, nc, t[:, 15, :], t[:, 12, :], t[:, 13, :], t[:, 3, :], bits[:, :])
            op(tt, t[:, 4, :], dt, aim, ALU.mult)
            magic, two_pi_hi, two_pi_lo, pi = 12582912.0, 6.28125, 0.0019353071795864769, 3.1415925
            op(ts, t[:, 9, :], t[:, 4, :], 0.15915494309189535, magic, ALU.mult, ALU.add)
            op(ts, t[:, 9, :], t[:, 9, :], -magic, None, ALU.add)
            op(ts, t[:, 10, :], t[:, 9, :], two_pi_hi, None, ALU.mult)
            op(tt, t[:, 10, :], t[:, 4, :], t[:, 10, :], ALU.subtract)
            op(ts, t[:, 9, :], t[:, 9, :], two_pi_lo, None, ALU.mult)
            op(tt, t[:, 10, :], t[:, 10, :], t[:, 9, :], ALU.subtract)
            op(ts, t[:, 5, :], t[:, 10, :], pi, -pi, ALU.min, ALU.max)
            op(ts, t[:, 11, :], t[:, 10, :], 1.5707963267948966, None, ALU.add)
            op(ts, t[:, 12, :], t[:, 11, :], 3.141592653589793, -6.283185307179586, ALU.is_gt, ALU.mult)
            op(tt, t[:, 11, :], t[:, 11, :], t[:, 12, :], ALU.add)
            op(ts, t[:, 6, :], t[:, 11, :], pi, -pi, ALU.min, ALU.max)
            dve.engine_nop().then_inc(reduced, 1)
            dve.wait_ge(sines, 1)
            mag, sin, cos = t[:, 3, :], t[:, 7, :], t[:, 8, :]
            pw = v.pw
            op(nc.vector.memset, pw[:, 0, 0, :], 1.0)
            op(nc.vector.memset, pw[:, 1, 0, :], 0.0)
            op(tt, pw[:, 0, 1, :], mag, cos, ALU.mult)
            op(tt, pw[:, 1, 1, :], mag, sin, ALU.mult)
            x, y = t[:, 9, :], t[:, 10, :]
            for n in range(2, 9):
                op(tt, x, pw[:, 0, n - 1, :], pw[:, 0, 1, :], ALU.mult)
                op(tt, y, pw[:, 1, n - 1, :], pw[:, 1, 1, :], ALU.mult)
                op(tt, pw[:, 0, n, :], x, y, ALU.subtract)
                op(tt, x, pw[:, 0, n - 1, :], pw[:, 1, 1, :], ALU.mult)
                op(tt, y, pw[:, 1, n - 1, :], pw[:, 0, 1, :], ALU.mult)
                op(tt, pw[:, 1, n, :], x, y, ALU.add)
            for n in range(8):
                nc.vector.tensor_copy(v.pwr[:, :, n, :], pw[:, :, 7 - n, :])
            op(nc.vector.tensor_copy, v.rot[:, 0, :], cos)
            op(nc.vector.tensor_copy, v.rot[:, 1, :], sin)
            op(nc.vector.tensor_copy, v.mag8[:, :], mag)
            for _ in range(3):
                op(tt, x, v.rot[:, 0, :], v.rot[:, 0, :], ALU.mult)
                op(tt, y, v.rot[:, 1, :], v.rot[:, 1, :], ALU.mult)
                op(tt, t[:, 13, :], v.rot[:, 0, :], v.rot[:, 1, :], ALU.mult)
                op(tt, v.rot[:, 0, :], x, y, ALU.subtract)
                op(ts, v.rot[:, 1, :], t[:, 13, :], 2.0, None, ALU.mult)
                op(tt, v.mag8[:, :], v.mag8[:, :], v.mag8[:, :], ALU.mult)
            op(tt, x, are, are, ALU.mult)
            op(tt, y, aim, aim, ALU.mult)
            op(tt, x, x, y, ALU.add)
            op(nc.vector.reciprocal, t[:, 11, :], x)
            op(ts, t[:, 12, :], pw[:, 0, 1, :], -1.0, None, ALU.add)
            op(tt, x, t[:, 12, :], are, ALU.mult)
            op(tt, y, pw[:, 1, 1, :], aim, ALU.mult)
            op(tt, x, x, y, ALU.add)
            op(tt, t[:, 14, :], x, t[:, 11, :], ALU.mult)
            op(tt, x, pw[:, 1, 1, :], are, ALU.mult)
            op(tt, y, t[:, 12, :], aim, ALU.mult)
            op(tt, x, x, y, ALU.subtract)
            op(tt, t[:, 15, :], x, t[:, 11, :], ALU.mult)
            qre, qim = [t[:, i, :].unsqueeze(2).broadcast_to([P, PAIRS, GC]) for i in (14, 15)]
            dve.wait_ge(b_in, 64)
            op(tt, v.bb[:, 0, :, :], braw[:, 0, :, :], qre, ALU.mult)
            op(tt, tb[:, :, :], braw[:, 1, :, :], qim, ALU.mult)
            op(tt, v.bb[:, 0, :, :], v.bb[:, 0, :, :], tb[:, :, :], ALU.subtract)
            op(tt, v.bb[:, 1, :, :], braw[:, 1, :, :], qre, ALU.mult)
            op(tt, tb[:, :, :], braw[:, 0, :, :], qim, ALU.mult)
            op(tt, v.bb[:, 1, :, :], v.bb[:, 1, :, :], tb[:, :, :], ALU.add)
            for i in range(2):
                for a in range(2):
                    b = k.bank[1 + 2 * i + a][:, :].rearrange("p (q h c) -> p q h c", h=2, c=GC)
                    for half in range(2):
                        at = slice(64 * half, 64 * half + 64)
                        nc.vector.tensor_copy(v.c[at, i, 16 * a:16 * a + 16, :], b[at, :, half, :])
            nc.vector.tensor_copy(v.h0[:, :, :, :], k.bank[5][:, :].rearrange("p (i b q) -> p i b q", i=2, b=NB))


def s5_weights(k, v, z):
    nc = k.nc
    S = lambda n: k.sem(f"s5w{z}_{n}")
    made, made_c, turned, off, kerned, k_off, placed, d_in = S("made"), S("made_c"), S("turned"), S("off"), S("kerned"), S("k_off"), S("placed"), S("d_in")
    q0 = z * QP
    with ExitStack() as ctx:
        ab = v.scratch[:, 0:2048].rearrange("p (i q t c) -> p i q t c", i=2, q=QP, c=GC)
        tmp = v.scratch[:, 2048:2048 + QP * 9 * GC].rearrange("p (q n c) -> p q n c", q=QP, c=GC)
        d16 = ctx.enter_context(nc.sbuf_tensor(f"s5w{z}_d", [GC, 2 * QP], F32))
        block = ctx.enter_context(nc.Block())

        @block.vector
        def _(dve):
            tt = nc.vector.tensor_tensor
            if z == 0:
                nc.vector.memset(v.toep[:, :, :], 0.0)
                nc.vector.memset(v.H[:, :, :, 0:1], 0.0)

            def product(dst, n, pw, x, i, j, k_, l, sub, scratch):
                def p(c):
                    return pw[:, c, 0:n, q0:q0 + QP].rearrange("p n q -> p q n").unsqueeze(3).broadcast_to([P, QP, n, GC])

                def y(c):
                    return x[:, c, q0:q0 + QP, :].unsqueeze(2).broadcast_to([P, QP, n, GC])
                tt(dst, p(i), y(j), ALU.mult)
                tt(scratch, p(k_), y(l), ALU.mult)
                dve.drain()
                return tt(dst, dst, scratch, ALU.subtract if sub else ALU.add)
            product(ab[:, 0], 8, v.pwr, v.bb, 0, 0, 1, 1, True, tmp[:, :, 0:8, :])
            dve.drain()
            product(ab[:, 1], 8, v.pwr, v.bb, 0, 1, 1, 0, False, tmp[:, :, 0:8, :])
            dve.drain().then_inc(made, 1)
            product(v.ca[:, 0], 9, v.pw, v.c, 0, 0, 1, 1, True, tmp[:, :, :, :])
            dve.drain()
            product(v.ca[:, 1], 9, v.pw, v.c, 0, 1, 1, 0, False, tmp[:, :, :, :])
            dve.drain()
            nc.vector.tensor_scalar(v.ca[:, 1], v.ca[:, 1], -1.0, None, ALU.mult)
            dve.drain().then_inc(made_c, 1)
            for i in range(4):
                dve.wait_ge(turned, i + 1)
                nc.vector.tensor_copy(v.wb[:, i // 2, 4 * (i % 2):4 * (i % 2) + 4, :], k.bank[i][:, :].rearrange("p (q n) -> p q n", q=4)).then_inc(off, 1)
            dve.wait_ge(d_in, 16)
            for i in range(4):
                dve.wait_ge(kerned, i + 1)
                g0 = 8 * (i // 2) + i % 2
                nc.vector.tensor_copy(v.kern[:, g0:g0 + 7:2, :], k.bank[4 + i][0:GC, :].rearrange("p (g n) -> p g n", g=4))
            dd = tmp[0:GC, :, :, :].rearrange("c q n e -> c (q n e)")[:, 0:2 * QP * GC].rearrange("c (g e) -> c g e", e=GC)
            tt(dd, k.ident[0:GC, 0:GC].unsqueeze(1).broadcast_to([GC, 2 * QP, GC]),
               d16[:, :].unsqueeze(2).broadcast_to([GC, 2 * QP, GC]), ALU.mult)
            dve.drain()
            tt(v.kern[:, :, 0:GC], v.kern[:, :, 0:GC], dd, ALU.add)
            dve.drain().then_inc(k_off, 1)

        @block.tensor
        def _(pe):
            pe.wait_ge(made, 1)
            for i in range(4):
                for q in range(4):
                    last = nc.tensor.transpose(k.bank[i][:, q * P:(q + 1) * P], ab[:, i // 2, 4 * (i % 2) + q].rearrange("p t c -> p (t c)"), k.ident[:, :])
                last.then_inc(turned, 1)
            pe.wait_ge(made_c, 1)
            for i in range(4):
                for j in range(4):
                    g = 8 * (i // 2) + 2 * j + i % 2
                    at, q = slice(64 * (g % 2), 64 * (g % 2) + 64), g // 2
                    for ri in range(2):
                        last = nc.tensor.matmul(k.bank[4 + i][0:GC, j * P:(j + 1) * P], v.bb[at, ri, q0 + q, :],
                                                v.ca[at, ri, q, 0:8, :].rearrange("p t c -> p (t c)"), start=ri == 0, stop=ri == 1)
                last.then_inc(kerned, 1)

        @block.sync
        def _(sp):
            with nc.allow_non_contiguous_dma(reason="a vector of 256 channels"):
                sp.dma_start(d16[:, :], k.w["s5_d"][0][z * 256:(z + 1) * 256].rearrange("(g c) -> c g", c=GC)).then_inc(d_in, 16)
            sp.wait_ge(k_off, 1)
            for t in range(Q5):
                sp.dma_start(v.toep[GC * t:GC * (t + 1), :, GC * t:P], v.kern[:, :, 0:P - GC * t]).then_inc(placed, 16)
            sp.wait_ge(placed, 16 * Q5)


def s5_scan(k, v, z, U, us, yr):
    nc = k.nc
    S = lambda n: k.sem(f"s5s{z}_{n}")
    sam_in, u_turned, u_off, driven, drive_off, scanned, y_done, y_off, table = (S("sam_in"), S("u_turned"), S("u_off"), S("driven"), S("drive_off"),
                                                                               S("scanned"), S("y_done"), S("y_off"), S("table"))
    ys_done, sam_zero = S("ys_done"), S("sam_zero")
    q0, c0 = z * QP, z * 256
    with ExitStack() as ctx:
        def sb(name, shape):
            return ctx.enter_context(nc.sbuf_tensor(f"s5s{z}_{name}", shape, F32))
        rc, rs, G = [v.scratch[:, 1024 * i:1024 * (i + 1)] for i in range(3)]
        rc, rs, G = rc.rearrange("p (q n) -> p q n", n=P), rs.rearrange("p (q n) -> p q n", n=P), G.rearrange("p (i q n) -> p i q n", i=2, n=P)
        A, B = [v.scratch[:, 3072 + 512 * i:3584 + 512 * i].rearrange("p (q n) -> p q n", n=P) for i in range(2)]
        uT = v.scratch[:, 4096:4096 + 16 * 144].rearrange("p (g n) -> p g n", g=16)
        pw2 = sb("pw2", [P, 4, QP])
        ta, tb, tc = sb("ta", [P, NB, QP]), sb("tb", [P, NB, QP]), sb("tc", [P, 2, NB, QP])
        block = ctx.enter_context(nc.Block())

        @block.sync
        def _(sp):
            sp.wait_ge(sam_zero, 1)
            for t in range(TS):
                sp.dma_start(v.u2[0:NB, :, t, :], us[t:NS:TS, c0:c0 + 256].rearrange("b (g c) -> b g c", c=GC)).then_inc(sam_in, 16)
                sp.dma_start(v.u2[NB:2 * NB, :, TS + t, :], us[t:NS:TS, c0:c0 + 256].rearrange("b (g c) -> b g c", c=GC)).then_inc(sam_in, 16)

        @block.tensor
        def _(pe):
            for i in range(4):
                if i >= 2:
                    pe.wait_ge(u_off, i - 1)
                for j in range(4):
                    g = 4 * i + j
                    last = nc.tensor.transpose(k.bank[i % 2][:, j * P:(j + 1) * P], U[:, z, g * P:(g + 1) * P], k.ident[:, :])
                last.then_inc(u_turned, 1)
            pe.wait_ge(sam_in, 16 * 2 * TS)
            for g in range(16):
                last = nc.tensor.transpose(k.bank[2][:, g * 16:(g + 1) * 16], v.u2[:, g, :, :].rearrange("b t c -> b (t c)"), k.ident[0:16, 0:16])
            last.then_inc(u_turned, 1)
            pe.wait_ge(u_off, 5)
            for i in range(2):
                for q in range(4):
                    for half in range(2):
                        g = 2 * (4 * i + q) + half
                        for ri in range(2):
                            last = nc.tensor.matmul(k.bank[4 + 2 * i + ri][64 * half:64 * half + 64, q * P:(q + 1) * P],
                                                    v.wb[:, ri, 4 * i + q, 64 * half:64 * half + 64], uT[:, g, 0:P], start=True, stop=True)
                last.then_inc(driven, 1)
            for q in range(QP):
                for half in range(2):
                    for ri in range(2):
                        last = nc.tensor.matmul(k.bank[3][64 * half:64 * half + 64, (ri * QP + q) * NB:(ri * QP + q + 1) * NB],
                                                v.wb[:, ri, q, 64 * half:64 * half + 64], uT[:, 2 * q + half, 136:144], start=True, stop=True)
            last.then_inc(driven, 1)
            for g in range(16):
                at, q = slice(64 * (g % 2), 64 * (g % 2) + 64), g // 2
                o = k.bank[g % 2][0:NB, q * 64:(q + 1) * 64]
                nc.tensor.matmul(o, uT[:, g, P:P + NB], v.toep[:, g, 0:64], start=True, stop=False)
                for ri in range(2):
                    last = nc.tensor.matmul(o, v.h0[at, ri, :, q0 + q], v.ca[at, ri, q, 1:5, :].rearrange("p t c -> p (t c)"),
                                            start=False, stop=ri == 1)
            last.then_inc(ys_done, 1)
            for i in range(4):
                pe.wait_ge(scanned, i // 2 + 1)
                if i == 0:
                    pe.wait_ge(drive_off, 3)
                    pe.wait_ge(y_off, 1)
                if i >= 2:
                    pe.wait_ge(y_off, i)
                for j in range(4):
                    g = 8 * (i // 2) + 2 * j + i % 2
                    at, q = slice(64 * (g % 2), 64 * (g % 2) + 64), g // 2
                    o = k.bank[i % 2][:, j * P:(j + 1) * P]
                    nc.tensor.matmul(o, uT[:, g, 0:P], v.toep[:, g, :], start=True, stop=False)
                    for ri in range(2):
                        last = nc.tensor.matmul(o, v.H[at, ri, q, 0:P], v.ca[at, ri, q, 1:9, :].rearrange("p t c -> p (t c)"), start=False, stop=ri == 1)
                last.then_inc(y_done, 1)

        @block.vector
        def _(dve):
            tt = nc.vector.tensor_tensor
            nc.vector.memset(v.u2[:, :, :, :], 0.0)
            dve.drain().then_inc(sam_zero, 1)
            for i in range(4):
                dve.wait_ge(u_turned, i + 1)
                nc.vector.tensor_copy(uT[:, 4 * i:4 * i + 4, 0:P], k.bank[i % 2][:, :].rearrange("p (g n) -> p g n", g=4)).then_inc(u_off, 1)
            dve.wait_ge(u_turned, 5)
            nc.vector.tensor_copy(uT[:, :, P:144], k.bank[2][:, 0:256].rearrange("p (g n) -> p g n", g=16)).then_inc(u_off, 1)
            nc.vector.memset(rc[:, :, 0:1], 1.0)
            nc.vector.memset(rs[:, :, 0:1], 0.0)
            nc.vector.tensor_copy(pw2[:, 0:2, :], v.rot[:, :, q0:q0 + QP])
            dve.drain()
            for j in range(7):
                n = 1 << j
                br, bi = [pw2[:, i, :].unsqueeze(2).broadcast_to([P, QP, n]) for i in range(2)]
                fa, fb = [x[:, :, :].rearrange("p a n -> p (a n)")[:, 0:QP * n].rearrange("p (q n) -> p q n", n=n) for x in (A, B)]
                tt(fa, rc[:, :, 0:n], br, ALU.mult)
                tt(fb, rs[:, :, 0:n], bi, ALU.mult)
                dve.drain()
                tt(rc[:, :, n:2 * n], fa, fb, ALU.subtract)
                dve.drain()
                tt(fa, rc[:, :, 0:n], bi, ALU.mult)
                tt(fb, rs[:, :, 0:n], br, ALU.mult)
                dve.drain()
                tt(rs[:, :, n:2 * n], fa, fb, ALU.add)
                tt(pw2[:, 2, :], pw2[:, 0, :], pw2[:, 0, :], ALU.mult)
                tt(pw2[:, 3, :], pw2[:, 1, :], pw2[:, 1, :], ALU.mult)
                dve.drain()
                tt(pw2[:, 1, :], pw2[:, 0, :], pw2[:, 1, :], ALU.mult)
                dve.drain()
                nc.vector.tensor_scalar(pw2[:, 1, :], pw2[:, 1, :], 2.0, None, ALU.mult)
                tt(pw2[:, 0, :], pw2[:, 2, :], pw2[:, 3, :], ALU.subtract)
                dve.drain()
            for i in range(2):
                c, s = rc[:, 4 * i:4 * i + 4, :], rs[:, 4 * i:4 * i + 4, :]
                er, ei = [k.bank[4 + 2 * i + ri][:, :].rearrange("p (q n) -> p q n", q=4) for ri in range(2)]
                dve.wait_ge(driven, i + 1)
                tt(A[:, :, :], er, c, ALU.mult)
                tt(B[:, :, :], ei, s, ALU.mult)
                dve.drain()
                tt(G[:, 0], A[:, :, :], B[:, :, :], ALU.add)
                dve.drain()
                tt(A[:, :, :], ei, c, ALU.mult)
                tt(B[:, :, :], er, s, ALU.mult)
                dve.drain()
                dve.engine_nop().then_inc(drive_off, 1)
                tt(G[:, 1], A[:, :, :], B[:, :, :], ALU.subtract)
                dve.drain()
                for ri in range(2):
                    for q in range(4):
                        nc.vector.tensor_tensor_scan(out=G[:, ri, q, :], data0=v.mag8[:, q0 + 4 * i + q:q0 + 4 * i + q + 1].broadcast_to([P, P]),
                                                     data1=G[:, ri, q, :], initial=0.0, op0=ALU.mult, op1=ALU.add)
                dve.drain()
                tt(A[:, :, :], G[:, 0], c, ALU.mult)
                tt(B[:, :, :], G[:, 1], s, ALU.mult)
                dve.drain()
                tt(v.H[:, 0, 4 * i:4 * i + 4, 1:P + 1], A[:, :, :], B[:, :, :], ALU.subtract)
                dve.drain()
                tt(A[:, :, :], G[:, 0], s, ALU.mult)
                tt(B[:, :, :], G[:, 1], c, ALU.mult)
                dve.drain()
                tt(v.H[:, 1, 4 * i:4 * i + 4, 1:P + 1], A[:, :, :], B[:, :, :], ALU.add)
                dve.drain().then_inc(scanned, 1)
            nc.vector.tensor_copy(v.fin[:, :, q0:q0 + QP], v.H[:, :, :, P])
            dve.wait_ge(driven, 3)
            hr, hi = v.h0[:, 0, :, q0:q0 + QP], v.h0[:, 1, :, q0:q0 + QP]
            a4r, a4i = [v.pw[:, ri, 4, q0:q0 + QP].unsqueeze(1).broadcast_to([P, NB, QP]) for ri in range(2)]
            d = k.bank[3][:, 0:2 * QP * NB].rearrange("p (i q b) -> p i b q", i=2, b=NB)
            nc.vector.tensor_copy(tc[:, :, :, :], d)
            dve.engine_nop().then_inc(drive_off, 1)
            for ri, (x, y, o) in enumerate(((hr, hi, ALU.subtract), (hi, hr, ALU.add))):
                tt(ta[:, :, :], x, a4r, ALU.mult)
                tt(tb[:, :, :], y, a4i, ALU.mult)
                dve.drain()
                tt(ta[:, :, :], ta[:, :, :], tb[:, :, :], o)
                dve.drain()
                tt(v.fs[:, ri, :, q0:q0 + QP], ta[:, :, :], tc[:, ri, :, :], ALU.add)
                dve.drain()
            dve.wait_ge(ys_done, 1)
            for i in range(2):
                nc.vector.tensor_copy(yr[:, :, c0:c0 + 256].rearrange("b t (q h c) -> b t q h c", h=2, c=GC)[:, :, :, i, :],
                                      k.bank[i][0:NB, :].rearrange("b (g t c) -> b t g c", t=TS, c=GC))
            dve.drain().then_inc(y_off, 1)
            for i in range(4):
                dve.wait_ge(y_done, i + 1)
                nc.vector.tensor_copy(U[:, z, :].rearrange("b (t n) -> b t n", t=Q5)[:, :, P * (i // 2):P * (i // 2 + 1)]
                                      .rearrange("b t (q h c) -> b t q h c", h=2, c=GC)[:, :, :, i % 2, :],
                                      k.bank[i % 2][:, :].rearrange("b (g t c) -> b t g c", t=Q5, c=GC)).then_inc(y_off, 1)


def s5_states_out(k, v):
    nc = k.nc
    turned, off, out = k.sem("s5o_turned"), k.sem("s5o_off"), k.sem("s5o_out")
    with ExitStack() as ctx:
        fp = ctx.enter_context(nc.sbuf_tensor("s5o_prompt", [PAIRS, 2, P], F32))
        fs = ctx.enter_context(nc.sbuf_tensor("s5o_sample", [P, 2, 2, P], F32))
        block = ctx.enter_context(nc.Block())

        @block.tensor
        def _(pe):
            for i in range(2):
                nc.tensor.transpose(k.bank[0][0:PAIRS, i * P:(i + 1) * P], v.fin[:, i, :], k.ident[:, :])
                for a in range(2):
                    last = nc.tensor.transpose(k.bank[1][:, (2 * i + a) * P:(2 * i + a + 1) * P],
                                               v.fs[:, i, 4 * a:4 * a + 4, :].rearrange("p b q -> p (b q)"), k.ident[:, :])
            last.then_inc(turned, 1)

        @block.vector
        def _(dve):
            dve.wait_ge(turned, 1)
            nc.vector.tensor_copy(fp[:, :, :], k.bank[0][0:PAIRS, 0:2 * P].rearrange("q (i n) -> q i n", i=2))
            nc.vector.tensor_copy(fs[:, :, :, :], k.bank[1][:, :].rearrange("q (i a n) -> q i a n", i=2, a=2))
            dve.drain().then_inc(off, 1)

        @block.sync
        def _(sp):
            sp.wait_ge(off, 1)
            for i, n in enumerate(("re", "im")):
                sp.dma_start(k.out[f"s5_{n}_prompt"][0, 0].rearrange("(q h) p -> q (h p)", h=2), fp[:, i, :]).then_inc(out, 16)
                sp.dma_start(k.out[f"s5_{n}_sample"][0].rearrange("(a b) (q h) p -> (b q) a (h p)", a=2, h=2), fs[:, i, :, :]).then_inc(out, 16)
            sp.wait_ge(out, 64)


def s5_gelu(k, U, yr, yT):
    nc = k.nc
    turned, off, squared, cubed, gate = k.sem("s5g_turned"), k.sem("s5g_off"), k.sem("s5g_sq"), k.sem("s5g_cubed"), k.sem("s5g_gate")
    with ExitStack() as ctx:
        t = ctx.enter_context(nc.sbuf_tensor("s5g_t", [P, 2, NT], F32))
        block = ctx.enter_context(nc.Block())

        @block.tensor
        def _(pe):
            for f in range(KD):
                for i in range(2):
                    n = 3 * f + i
                    if n >= 4:
                        pe.wait_ge(off, n - 3)
                    for j in range(4):
                        last = nc.tensor.transpose(k.bank[n % 4][:, j * P:(j + 1) * P], U[:, f // 2, (4 * i + j) * 256 + (f % 2) * P:(4 * i + j) * 256 + (f % 2 + 1) * P], k.ident[:, :])
                    last.then_inc(turned, 1)
                n = 3 * f + 2
                if n >= 4:
                    pe.wait_ge(off, n - 3)
                for t_ in range(TS):
                    last = nc.tensor.transpose(k.bank[n % 4][:, t_ * NB:(t_ + 1) * NB], yr[:, t_, f * P:(f + 1) * P], k.ident[0:NB, 0:NB])
                last.then_inc(turned, 1)

        @block.vector
        def _(dve):
            for f in range(KD):
                for i in range(2):
                    n = 3 * f + i
                    dve.wait_ge(turned, n + 1)
                    nc.vector.tensor_copy(yT[:, f, 0:SEQ].rearrange("p (c t) -> p t c", t=Q5)[:, 4 * i:4 * i + 4, :],
                                          k.bank[n % 4][:, :].rearrange("p (t c) -> p t c", t=4)).then_inc(off, 1)
                n = 3 * f + 2
                dve.wait_ge(turned, n + 1)
                nc.vector.tensor_copy(yT[:, f, SEQ:NT].rearrange("p (b t) -> p t b", t=TS),
                                      k.bank[n % 4][:, 0:NS].rearrange("p (t b) -> p t b", t=TS)).then_inc(off, 1)
                dve.wait_ge(squared, f + 1)
                nc.vector.tensor_scalar(t[:, f % 2, :], t[:, f % 2, :], 0.044715, 1.0, ALU.mult, ALU.add)
                dve.drain()
                nc.vector.tensor_tensor(t[:, f % 2, :], t[:, f % 2, :], yT[:, f, :], ALU.mult).then_inc(cubed, 1)
                dve.wait_ge(gate, f + 1)
                nc.vector.tensor_tensor(yT[:, f, :], yT[:, f, :], t[:, f % 2, :], ALU.mult)
                dve.drain()

        @block.scalar
        def _(act):
            for f in range(KD):
                act.wait_ge(off, 3 * f + 3)
                nc.scalar.activation(t[:, f % 2, :], yT[:, f, :], ACT.Square).then_inc(squared, 1)
                act.wait_ge(cubed, f + 1)
                nc.scalar.activation(t[:, f % 2, :], t[:, f % 2, :], ACT.Sigmoid, scale=1.5957691216057308).then_inc(gate, 1)


def s5(k, yT):
    nc = k.nc
    v = Kernel()
    v.scratch = yT[:, :, :].rearrange("p a t -> p (a t)")
    with ExitStack() as ctx:
        def sb(name, shape):
            return ctx.enter_context(nc.sbuf_tensor(f"s5_{name}", shape, F32))
        U, us, yr = sb("u", [P, 4, 16 * P]), sb("u_sample", [NS, D]), sb("y_sample", [NB, TS, D])
        xn_scope = ExitStack()
        xnT = xn_scope.enter_context(nc.sbuf_tensor("s5_xnT", [P, KD, NT], F32))
        move(k, "s5_xn", xnT[:, :, :], k.xn_dram)
        lhs = [((lambda q, t=t: xnT[:, q, t:SEQ:Q5]), P) for t in range(Q5)] + [((lambda q: xnT[:, q, SEQ:NT]), NS)]

        def evac(dve, i, s, ps):
            if i == Q5:
                return nc.vector.tensor_copy(us[:, s * 512:(s + 1) * 512], ps)
            dst = U[:, 2 * s:2 * s + 2, :].rearrange("p z (g t c) -> p (z g) t c", t=Q5, c=GC)[:, :, i, :]
            return nc.vector.tensor_copy(dst, ps.rearrange("p (g c) -> p g c", c=GC))
        gemm_rows(k, "s5u", k.w_in[:, C_S:C_S + D], lhs, evac)
        xn_scope.close()
        with ExitStack() as inner:
            def sb(name, shape):
                return inner.enter_context(nc.sbuf_tensor(f"s5_{name}", shape, F32))
            v.pw, v.pwr, v.rot, v.mag8 = sb("pw", [P, 2, 9, PAIRS]), sb("pwr", [P, 2, 8, PAIRS]), sb("rot", [P, 2, PAIRS]), sb("mag8", [P, PAIRS])
            v.bb, v.c, v.h0 = sb("bb", [P, 2, PAIRS, GC]), sb("c", [P, 2, PAIRS, GC]), sb("h0", [P, 2, NB, PAIRS])
            v.fin, v.fs = sb("fin", [P, 2, PAIRS]), sb("fs", [P, 2, NB, PAIRS])
            s5_params(k, v)
            v.ca, v.H = sb("ca", [P, 2, QP, 9, GC]), sb("H", [P, 2, QP, P + 1])
            r0, r1 = k.ring[:, 0, :], k.ring[:, 1, :]
            v.toep = r0[:, 0:2048].rearrange("p (g n) -> p g n", g=16)
            v.wb = r0[:, 2048:4096].rearrange("p (i q n) -> p i q n", i=2, q=QP)
            v.kern = r1[0:GC, 0:2048].rearrange("p (g n) -> p g n", g=16)
            v.u2 = r1[0:2 * NB, 2048:4096].rearrange("p (g t c) -> p g t c", t=Q5, c=GC)
            for z in range(4):
                s5_weights(k, v, z)
                s5_scan(k, v, z, U, us, yr)
            s5_states_out(k, v)
        s5_gelu(k, U, yr, yT)
        release(k)


RP = 8
RC = 64
RN = SEQ // RC
KAPPA = 0.6065306597126334
BATCH = 4


def rwkv_masks(k, v):
    nc = k.nc
    ones_made, made = k.sem("rm_ones"), k.sem("rm_made")
    with nc.Block() as block:
        @block.vector
        def _(dve):
            for t in (v.m_in, v.m_cross, v.m_lower, v.m_out, v.reset):
                nc.vector.memset(t[:, :], 1.0)
            dve.drain()
            nc.vector.memset(v.reset[:, 0:SEQ // 2:RC], 0.0)
            for half in range(2):
                at = slice(64 * half, 64 * half + 64)
                nc.vector.tensor_copy(v.m_out[at, P:P + RC], k.upper[at, at])
            dve.drain().then_inc(ones_made, 1)

        @block.gpsimd
        def _(pool):
            pool.wait_ge(ones_made, 1)

            def keep(at, pattern, base, mult):
                pool.affine_select(out=at, in_=at, compare_op=ALU.is_ge, fill=0.0, base=base, pattern=pattern, channel_multiplier=mult)
                pool.drain()

            def blocks(t):
                return t[:, :].rearrange("p (a c) -> p a c", c=16)
            for t in (v.m_in, v.m_lower):
                keep(blocks(t), [[-16, 8], [0, 16]], 0, 1)
                keep(blocks(t), [[16, 8], [0, 16]], 15, -1)
            keep(v.m_in[:, :], [[1, P]], -1, -1)
            keep(v.m_lower[:, :], [[-1, P]], -1, 1)
            keep(blocks(v.m_cross), [[16, 8], [0, 16]], -1, -1)
            keep(v.m_out[:, 0:P], [[1, P]], -1, -1)


def rwkv_lora(k, v):
    nc = k.nc
    in_, w_in, mixed = k.sem("rl_in"), k.sem("rl_w_in"), k.sem("rl_mixed")
    with nc.sbuf_tensor("rl_raw", [P, 2, 1 + SEQ], F32) as raw, nc.sbuf_tensor("rl_d", [P, 2, SEQ], F32) as d, nc.Block() as block:
        @block.sync
        def _(sp):
            sp.dma_start(raw[:, :, 1:1 + SEQ], k.proj[24 * P:26 * P, 0:SEQ].rearrange("(a p) t -> p a t", p=P)).then_inc(in_, 16)
            sp.dma_start(v.w2a2[0:64, :], k.w["rwkv_w2"][0]).then_inc(w_in, 16)
            sp.dma_start(v.w2a2[64:128, :], k.w["rwkv_a2"][0]).then_inc(w_in, 16)
            sp.dma_start(v.g2[:, :], k.w["rwkv_g2"][0]).then_inc(w_in, 16)
            sp.wait_ge(w_in, 48)

        @block.vector
        def _(dve):
            nc.vector.memset(raw[:, :, 0:1], 0.0)
            dve.wait_ge(in_, 16)
            dve.drain()
            for i in range(2):
                nc.vector.tensor_tensor(d[:, i, :], raw[:, i, 0:SEQ], raw[:, i, 1:1 + SEQ], ALU.subtract)
            dve.drain()
            for i in range(2):
                mu = k.col["rwkv_mu"][:, 24 + i:25 + i]
                nc.vector.scalar_tensor_tensor(out=v.lora[:, i, :], in0=d[:, i, :], scalar=mu, in1=raw[:, i, 1:1 + SEQ], op0=ALU.mult, op1=ALU.add)
            dve.drain().then_inc(mixed, 1)

        @block.scalar
        def _(act):
            act.wait_ge(mixed, 1)
            nc.scalar.activation(v.lora[0:64, 0, :], v.lora[0:64, 0, :], ACT.Tanh)
            nc.scalar.activation(v.lora[:, 1, :], v.lora[:, 1, :], ACT.Sigmoid)


def rwkv_prepare(k, v, j):
    nc = k.nc
    S = lambda n: k.sem(f"rp{j}_{n}")
    in_, mixed, lw, la, cum, a_ready = S("in"), S("mixed"), S("lw"), S("la"), S("cum"), S("a_ready")
    k_sq, k_sum, k_rs, exps, prods, bon, bon_sum, w_sig = S("k_sq"), S("k_sum"), S("k_rs"), S("exps"), S("prods"), S("bon"), S("bon_sum"), S("w_sig")
    col = k.col
    raw, pm, T = v.raw, v.pm, v.T
    r, kk0, val = pm[:, 0, :], pm[:, 1, :], pm[:, 2, :]
    with nc.Block() as block:
        @block.sync
        def _(sp):
            for i in range(3):
                row = (i * 8 + j) * P
                sp.dma_start(raw[:, i, 1:1 + SEQ], k.proj[row:row + P, 0:SEQ]).then_inc(in_, 16)

        @block.tensor
        def _(pe):
            for t in range(2):
                nc.tensor.matmul(k.bank[t][:, :], v.w2a2[0:64, j * P:(j + 1) * P], v.lora[0:64, 0, t * 512:(t + 1) * 512], start=True, stop=True)
            for t in range(2):
                last = nc.tensor.matmul(k.bank[2 + t][:, :], v.w2a2[64:128, j * P:(j + 1) * P], v.lora[64:128, 0, t * 512:(t + 1) * 512],
                                        start=True, stop=True)
            last.then_inc(lw, 1)
            pe.wait_ge(k_sq, 1)
            for t in range(2):
                last = nc.tensor.matmul(k.bank[4 + t][:, :], k.ones64[:, :], T[5][:, t * 512:(t + 1) * 512], start=True, stop=True)
            last.then_inc(k_sum, 1)
            pe.wait_ge(bon, 1)
            for t in range(2):
                last = nc.tensor.matmul(k.bank[6 + t][:, :], k.ones64[:, :], T[6][:, t * 512:(t + 1) * 512], start=True, stop=True)
            last.then_inc(bon_sum, 1)

        @block.scalar
        def _(act):
            act.wait_ge(lw, 1)
            for t in range(2):
                nc.scalar.activation(T[0][:, t * 512:(t + 1) * 512], k.bank[t][:, :], ACT.Sigmoid, bias=col["rwkv_w0"][:, j:j + 1])
            act.drain().then_inc(w_sig, 1)
            for t in range(2):
                nc.scalar.activation(T[2][:, t * 512:(t + 1) * 512], k.bank[2 + t][:, :], ACT.Sigmoid, bias=col["rwkv_a0"][:, j:j + 1])
            act.drain().then_inc(a_ready, 1)
            act.wait_ge(mixed, 1)
            nc.scalar.activation(T[5][:, :], kk0, ACT.Square, scale=col["rwkv_k_k"][:, j:j + 1])
            act.drain().then_inc(k_sq, 1)
            act.wait_ge(cum, 1)
            nc.scalar.activation(T[3][:, :], T[1][:, :], ACT.Exp, scale=-KAPPA)
            nc.scalar.activation(T[4][:, :], T[1][:, :], ACT.Exp, scale=KAPPA)
            act.wait_ge(k_sum, 1)
            for t in range(2):
                nc.scalar.activation(T[5][:, t * 512:(t + 1) * 512], k.bank[4 + t][:, :], ACT.Ln, bias=k.eps[:, 1:2])
            act.drain()
            nc.scalar.activation(T[5][:, :], T[5][:, :], ACT.Exp, scale=-0.5)
            act.wait_ge(prods, 1)
            nc.scalar.activation(T[0][:, :], T[0][:, :], ACT.Exp, scale=-KAPPA)
            act.drain().then_inc(exps, 1)

        @block.vector
        def _(dve):
            tt, ts, stt = nc.vector.tensor_tensor, nc.vector.tensor_scalar, nc.vector.scalar_tensor_tensor
            nc.vector.memset(raw[:, :, 0:1], 0.0)
            dve.wait_ge(in_, 48)
            dve.drain()
            for i in range(3):
                tt(T[7][:, :], raw[:, i, 0:SEQ], raw[:, i, 1:1 + SEQ], ALU.subtract)
                dve.drain()
                stt(out=pm[:, i, :], in0=T[7][:, :], scalar=col["rwkv_mu"][:, i * 8 + j:i * 8 + j + 1], in1=raw[:, i, 1:1 + SEQ],
                    op0=ALU.mult, op1=ALU.add)
                dve.drain()
            dve.engine_nop().then_inc(mixed, 1)
            dve.wait_ge(w_sig, 1)
            chunked = lambda x: x.rearrange("p (c t) -> p c t", t=RC)
            for half in (slice(0, SEQ // 2), slice(SEQ // 2, SEQ)):
                nc.vector.tensor_tensor_scan(out=T[1][:, half], data0=v.reset[:, :], data1=T[0][:, half], initial=0.0, op0=ALU.mult, op1=ALU.add)
            dve.drain().then_inc(cum, 1)
            tt(T[0][:, :], T[1][:, :], T[0][:, :], ALU.subtract)
            dve.wait_ge(a_ready, 1)
            ts(T[7][:, :], T[2][:, :], -1.0, col["rwkv_k_a"][:, j:j + 1], ALU.add, ALU.mult)
            dve.drain()
            stt(out=T[7][:, :], in0=T[7][:, :], scalar=1.0, in1=kk0, op0=ALU.add, op1=ALU.mult)
            dve.drain()
            stt(out=T[6][:, :], in0=r, scalar=col["rwkv_r_k"][:, j:j + 1], in1=T[7][:, :], op0=ALU.mult, op1=ALU.mult)
            dve.drain().then_inc(bon, 1)
            dve.engine_nop().then_inc(prods, 1)
            dve.wait_ge(exps, 1)
            halves = [(slice(64 * h, 64 * h + 64), slice(64 * h, 64 * h + 64)) for h in range(2)]
            tt(v.AR[:, :, P:P + RC], chunked(r), chunked(T[3][:, :]), ALU.mult)
            nc.vector.tensor_copy(v.PC[:, :], chunked(T[3][:, :])[:, :, RC - 1])
            stt(out=T[1][:, :], in0=kk0, scalar=col["rwkv_k_k"][:, j:j + 1], in1=T[5][:, :], op0=ALU.mult, op1=ALU.mult)
            dve.drain()
            tt(T[2][:, :], T[2][:, :], T[4][:, :], ALU.mult)
            dve.drain()
            for at, to in halves:
                stt(out=v.AR[at, :, to], in0=chunked(T[1][at, :]), scalar=-1.0, in1=chunked(T[0][at, :]), op0=ALU.mult, op1=ALU.mult)
                tt(v.B[at, :, to], chunked(T[1][at, :]), chunked(T[2][at, :]), ALU.mult)
                tt(v.K[at, :, to], chunked(T[7][at, :]), chunked(T[4][at, :]), ALU.mult)
                nc.vector.tensor_copy(v.V[at, :, to], chunked(val[at, :]))
            dve.wait_ge(bon_sum, 1)
            dve.drain()
            for t in range(2):
                at = slice(t * 512, (t + 1) * 512)
                tt(v.bonus[:, at], k.bank[6 + t][:, :], val[:, at], ALU.mult)


INVERSION = [("gram", "v"), ("rows", "va"), ("square", "va"), ("fourth", "va"), ("eighth", "v"), ("by4", "v"), ("by2", "v"), ("by1", "v"),
             ("turn", "va"), ("cross1", "v"), ("cross2", "v"), ("cross3", "v")]


def rwkv_invert(k, v, j):
    nc = k.nc
    S = lambda n: k.sem(f"ri{j}_{n}")
    pes, vs, as_ = [S("pe0"), S("pe1")], [S("dve0"), S("dve1")], [S("act0"), S("act1")]
    per = {"v": sum("v" in w for _, w in INVERSION), "a": sum("a" in w for _, w in INVERSION)}

    def done(n, s, who):
        return n * per[who] + sum(who in w for _, w in INVERSION[:s + 1])

    rounds = RN // BATCH // 2
    with nc.Block() as block:
        def b(p, i):
            return k.bank[4 * p + i]

        @block.tensor
        def _(pe):
            mm = nc.tensor.matmul
            for n in range(rounds):
                for s, (step, who) in enumerate(INVERSION):
                    for p in range(2):
                        x, c0 = v.inv[p], (2 * n + p) * BATCH
                        for w, sem in (("v", vs[p]), ("a", as_[p])):
                            m = done(n, s - 1, w) if s else n * per[w]
                            if m:
                                pe.wait_ge(sem, m)
                        for i in range(BATCH):
                            c, q = c0 + i, slice(i * P, (i + 1) * P)
                            if step == "gram":
                                o = slice((i % 2) * 192, (i % 2) * 192 + 192)
                                mm(b(p, i // 2)[:, o], v.B[:, c, :], v.AR[:, c, :], start=True, stop=True)
                                last = mm(b(p, 2 + i // 2)[:, o], v.K[:, c, :], v.AR[:, c, :], start=True, stop=True)
                            elif step == "rows":
                                mm(b(p, 0)[:, q], v.AR[:, c, 0:P], v.B[:, c, :], start=True, stop=True)
                                for y, t in ((v.B, 1), (v.K, 2), (v.V, 3)):
                                    last = nc.tensor.transpose(b(p, t)[:, q], y[:, c, :], k.ident[:, :])
                            elif step == "square":
                                mm(b(p, 0)[:, q], x.A[:, i, :], x.D[:, i, :], start=True, stop=True)
                                last = mm(b(p, 1)[:, q], x.D[:, i, :], x.A[:, i, :], start=True, stop=True)
                            elif step == "fourth":
                                mm(b(p, 2)[:, q], x.A2[:, i, :], x.D2[:, i, :], start=True, stop=True)
                                last = mm(b(p, 3)[:, q], x.D2[:, i, :], x.A2[:, i, :], start=True, stop=True)
                            elif step == "eighth":
                                last = mm(b(p, 0)[:, q], x.A4[:, i, :], x.D4[:, i, :], start=True, stop=True)
                            elif step == "by4":
                                last = mm(b(p, 1)[:, q], x.A4[:, i, :], x.X[:, i, :], start=True, stop=True)
                            elif step == "by2":
                                last = mm(b(p, 2)[:, q], x.A2[:, i, :], x.X[:, i, :], start=True, stop=True)
                            elif step == "by1":
                                last = mm(b(p, 3)[:, q], x.A[:, i, :], x.X[:, i, :], start=True, stop=True)
                            elif step == "turn":
                                mm(b(p, 0)[:, q], x.O[:, i, :], x.X[:, i, :], start=True, stop=True)
                                last = nc.tensor.transpose(b(p, 1)[:, q], x.X[:, i, :], k.ident[:, :])
                            else:
                                y = x.G if step == "cross1" else v.N[:, c0:c0 + BATCH]
                                last = mm(b(p, 2 + s % 2)[:, q], x.F[:, i, :], y[:, i, :], start=True, stop=True)
                        last.then_inc(pes[p], 1)

        def view(bank):
            return bank[:, :].rearrange("p (i n) -> p i n", n=P)

        @block.vector
        def _(dve):
            tt = nc.vector.tensor_tensor

            def mask(m, n=BATCH):
                return m.unsqueeze(1).broadcast_to([P, n, m.shape[1]])
            for n in range(rounds):
                for s, (step, who) in enumerate(INVERSION):
                    for p in range(2):
                        x, c0 = v.inv[p], (2 * n + p) * BATCH
                        if "v" not in who:
                            continue
                        dve.wait_ge(pes[p], n * len(INVERSION) + s + 1)
                        if step == "gram":
                            for h in range(2):
                                i, c = slice(2 * h, 2 * h + 2), slice(c0 + 2 * h, c0 + 2 * h + 2)
                                g = b(p, h)[:, 0:384].rearrange("p (i n) -> p i n", n=192)
                                tt(x.A[:, i, :], g[:, :, 0:P], mask(v.m_in[:, :], 2), ALU.mult)
                                tt(x.O[:, i, :], g[:, :, 0:P], mask(v.m_cross[:, :], 2), ALU.mult)
                                tt(v.BR[:, c, :], g[:, :, P:192], mask(v.m_out[:, P:192], 2), ALU.mult)
                                g = b(p, 2 + h)[:, 0:384].rearrange("p (i n) -> p i n", n=192)
                                last = tt(v.KX[:, c, :], g, mask(v.m_out[:, :], 2), ALU.mult)
                        elif step == "rows":
                            last = tt(x.D[:, :, :], view(b(p, 0)), mask(v.m_lower[:, :]), ALU.mult)
                        elif step == "square":
                            last = nc.vector.tensor_copy(x.D2[:, :, :], view(b(p, 0)))
                        elif step == "fourth":
                            last = nc.vector.tensor_copy(x.D4[:, :, :], view(b(p, 2)))
                        elif step == "eighth":
                            last = tt(x.X[:, :, :], view(b(p, 0)), mask(k.ident[:, :]), ALU.add)
                        elif step in ("by4", "by2", "by1"):
                            bank = {"by4": 1, "by2": 2, "by1": 3}[step]
                            last = tt(x.X[:, :, :], view(b(p, bank)), x.X[:, :, :], ALU.add)
                        elif step == "turn":
                            last = nc.vector.tensor_copy(x.F[:, :, :], view(b(p, 0)))
                        else:
                            last = tt(v.N[:, c0:c0 + BATCH, :], view(b(p, 2 + s % 2)), x.G[:, :, :], ALU.add)
                        last.then_inc(vs[p], 1)

        @block.scalar
        def _(act):
            copy = lambda dst, src: nc.scalar.activation(dst, src, ACT.Copy)
            for n in range(rounds):
                for s, (step, who) in enumerate(INVERSION):
                    for p in range(2):
                        x, c0 = v.inv[p], (2 * n + p) * BATCH
                        if "a" not in who:
                            continue
                        act.wait_ge(pes[p], n * len(INVERSION) + s + 1)
                        if step == "rows":
                            for y, t in ((v.B, 1), (v.K, 2), (v.V, 3)):
                                last = copy(y[:, c0:c0 + BATCH, :], view(b(p, t)))
                        elif step == "square":
                            last = copy(x.A2[:, :, :], view(b(p, 1)))
                        elif step == "fourth":
                            last = copy(x.A4[:, :, :], view(b(p, 3)))
                        else:
                            last = copy(x.G[:, :, :], view(b(p, 1)))
                        last.then_inc(as_[p], 1)


def rwkv_scan(k, v, j):
    nc = k.nc
    S_ = lambda n: k.sem(f"rs{j}_{n}")
    r_mm, r_off, u_mm, u_off, s_mm, s_off, y_mm, y_off, decayed, turned, t_off, out = (
        S_("r_mm"), S_("r_off"), S_("u_mm"), S_("u_off"), S_("s_mm"), S_("s_off"), S_("y_mm"), S_("y_off"), S_("decayed"), S_("turned"),
        S_("t_off"), S_("out"))
    with nc.Block() as block:
        @block.tensor
        def _(pe):
            mm = nc.tensor.matmul
            for c in range(RN):
                o = k.bank[4 + (c // 8)][:, (c % 8) * RC:(c % 8 + 1) * RC]
                mm(k.bank[0][:, 0:P], v.KX[:, c, 0:P], v.V[:, c, :], start=True, stop=False)
                pe.wait_ge(s_off, c + 1)
                mm(k.bank[0][:, 0:P], v.AR[:, c, 0:P], v.ST[:, c % 2, :], start=False, stop=True).then_inc(r_mm, 1)
                mm(o, v.V[:, c, :], v.KX[:, c, P:192], start=True, stop=False)
                mm(o, v.ST[:, c % 2, :], v.AR[:, c, P:192], start=False, stop=False)
                mm(k.bank[2][:, 0:P], v.K[:, c, :], v.V[:, c, :], start=True, stop=False)
                pe.wait_ge(r_off, c + 1)
                mm(k.bank[1][:, 0:P], v.N[:, c, :], v.R[:, :], start=True, stop=True).then_inc(u_mm, 1)
                pe.wait_ge(u_off, c + 1)
                mm(k.bank[2][:, 0:P], v.B[:, c, :], v.U[:, :], start=False, stop=True).then_inc(s_mm, 1)
                mm(o, v.U[:, :], v.BR[:, c, :], start=False, stop=True).then_inc(y_mm, 1)
            pe.wait_ge(s_off, RN + 1)
            nc.tensor.transpose(k.bank[3][:, 0:P], v.ST[:, RN % 2, :], k.ident[:, :]).then_inc(turned, 1)

        @block.vector
        def _(dve):
            nc.vector.memset(v.ST[:, 0, :], 0.0)
            dve.drain().then_inc(s_off, 1)
            for c in range(RN):
                nc.vector.tensor_scalar(v.SD[:, :], v.ST[:, c % 2, :], v.PC[:, c:c + 1], None, ALU.mult)
                dve.wait_ge(r_mm, c + 1)
                nc.vector.tensor_copy(v.R[:, :], k.bank[0][:, 0:P]).then_inc(r_off, 1)
                dve.wait_ge(s_mm, c + 1)
                dve.drain()
                nc.vector.scalar_tensor_tensor(out=v.ST[:, (c + 1) % 2, :], in0=k.bank[2][:, 0:P], scalar=v.PC[:, c:c + 1], in1=v.SD[:, :],
                                               op0=ALU.mult, op1=ALU.add).then_inc(s_off, 1)
                dve.drain()
            dve.wait_ge(turned, 1)
            nc.vector.tensor_copy(v.SD[:, :], k.bank[3][:, 0:P]).then_inc(t_off, 1)

        @block.scalar
        def _(act):
            for c in range(RN):
                act.wait_ge(u_mm, c + 1)
                nc.scalar.activation(v.U[:, :], k.bank[1][:, 0:P], ACT.Copy).then_inc(u_off, 1)
            for i in range(2):
                act.wait_ge(y_mm, 8 * i + 8)
                nc.scalar.activation(v.y[:, i * 512:(i + 1) * 512], k.bank[4 + i][:, :], ACT.Copy)

        @block.sync
        def _(sp):
            sp.wait_ge(t_off, 1)
            for h in range(2):
                at = slice(64 * h, 64 * h + 64)
                sp.dma_start(k.out["rwkv_prompt"][0, 0, 2 * j + h], v.SD[at, at]).then_inc(out, 16)
            sp.wait_ge(out, 32)


def rwkv_finish(k, tag, y, bonus, gate, dst, n, ln_w, ln_b, T):
    nc = k.nc
    S = lambda name: k.sem(f"{tag}_{name}")
    summed, centred, squared, varsum, rstd, g_off = S("summed"), S("centred"), S("squared"), S("varsum"), S("rstd"), S("g_off")
    parts = [(i, i * 512, min(512, n - i * 512)) for i in range((n + 511) // 512)]
    with nc.Block() as block:
        @block.tensor
        def _(pe):
            for i, t0, m in parts:
                last = nc.tensor.matmul(k.bank[2 + i][:, 0:m], k.ones64[:, :], y[:, t0:t0 + m], start=True, stop=True)
            last.then_inc(summed, 1)
            gate(pe).then_inc(g_off, 1)
            pe.wait_ge(squared, 1)
            for i, t0, m in parts:
                last = nc.tensor.matmul(k.bank[4 + i][:, 0:m], k.ones64[:, :], T[0][:, t0:t0 + m], start=True, stop=True)
            last.then_inc(varsum, 1)

        @block.vector
        def _(dve):
            tt, ts, stt = nc.vector.tensor_tensor, nc.vector.tensor_scalar, nc.vector.scalar_tensor_tensor
            dve.wait_ge(summed, 1)
            for i, t0, m in parts:
                stt(out=y[:, t0:t0 + m], in0=k.bank[2 + i][:, 0:m], scalar=-1.0 / 64, in1=y[:, t0:t0 + m], op0=ALU.mult, op1=ALU.add)
            dve.drain().then_inc(centred, 1)
            dve.wait_ge(rstd, 1)
            tt(y, y, T[1][:, 0:n], ALU.mult)
            dve.drain()
            if ln_w.shape[1] == 1:
                ts(y, y, ln_w, ln_b, ALU.mult, ALU.add)
            else:
                tt(y, y, ln_w, ALU.mult)
                dve.drain()
                tt(y, y, ln_b, ALU.add)
            dve.drain()
            tt(y, y, bonus, ALU.add)
            dve.wait_ge(g_off, 1)
            dve.drain()
            for i, t0, m in parts:
                d = dst(t0, m)
                tt(d, y[:, t0:t0 + m].rearrange("p (a t) -> p a t", a=d.shape[1]), k.bank[i][:, 0:m].rearrange("p (a t) -> p a t", a=d.shape[1]),
                   ALU.mult)

        @block.scalar
        def _(act):
            act.wait_ge(centred, 1)
            nc.scalar.activation(T[0][:, 0:n], y, ACT.Square)
            act.drain().then_inc(squared, 1)
            act.wait_ge(varsum, 1)
            for i, t0, m in parts:
                nc.scalar.activation(T[1][:, t0:t0 + m], k.bank[4 + i][:, 0:m], ACT.Ln, bias=k.eps[:, 2:3], scale=1.0 / 64)
            act.drain()
            nc.scalar.activation(T[1][:, 0:n], T[1][:, 0:n], ACT.Exp, scale=-0.5)
            act.drain().then_inc(rstd, 1)


def rwkv_samples(k, v, yT):
    nc = k.nc
    W = RP * NS
    S = lambda n: k.sem(f"rx_{n}")
    rows_in, raw_in, turned, off, mixed, acted, lw, sig, k_sq, k_sum, k_rs = (S("rows_in"), S("raw_in"), S("turned"), S("off"), S("mixed"), S("acted"),
                                                                             S("lw"), S("sig"), S("k_sq"), S("k_sum"), S("k_rs"))
    bon, bon_sum, vec_made, tok_turned, tok_off, stored, loaded = S("bon"), S("bon_sum"), S("vec_made"), S("tok_turned"), S("tok_off"), S("stored"), S("loaded")
    with ExitStack() as keep:
        def sbk(name, shape):
            return keep.enter_context(nc.sbuf_tensor(f"rx_{name}", shape, F32))
        yrow, bonus, lora = sbk("yrow", [NS, D]), sbk("bonus", [P, RP, NS]), sbk("lora", [P, 2, NS])
        with ExitStack() as ctx:
            def sb(name, shape):
                return ctx.enter_context(nc.sbuf_tensor(f"rx_{name}", shape, F32))
            srow = k.ring[0:NB, 0, 0:R_COLS]
            ext, pm, d = sb("ext", [P, RT, NB, 5]), sb("pm", [P, RT, NS]), sb("d", [P, RT, NS])
            T = [sb(f"T{i}", [P, RP, NS]) for i in range(10)]
            tok = k.ring[0:NS, :, :].rearrange("s a n -> s (a n)")[:, 0:6 * D]
            six = [pm[:, 0:8, :], T[0], T[7], pm[:, 16:24, :], T[9], T[8]]
            block = ctx.enter_context(nc.Block())

            def vec(name):
                return k.col[name].unsqueeze(2).broadcast_to([P, RP, NS])

            @block.sync
            def _(sp):
                sp.dma_start(srow, k.w["state_rwkv_shift"][0]).then_inc(rows_in, 16)
                for b in range(NB):
                    sp.dma_start(ext[:, :, b, 1:5], k.proj[0:R_COLS, SEQ + TS * b:SEQ + TS * b + TS].rearrange("(a p) t -> p a t", p=P)).then_inc(raw_in, 16)
                sp.wait_ge(tok_off, 12)
                sp.dma_start(k.vec_dram.rearrange("s a c -> s (a c)"), tok).then_inc(stored, 16)
                sp.wait_ge(stored, 16)

            @block.tensor
            def _(pe):
                pe.wait_ge(rows_in, 16)
                for a in range(RT):
                    last = nc.tensor.transpose(k.bank[0][:, a * NB:(a + 1) * NB], srow[:, a * P:(a + 1) * P], k.ident[0:NB, 0:NB])
                last.then_inc(turned, 1)
                pe.wait_ge(acted, 1)
                for j in range(RP):
                    last = nc.tensor.matmul(k.bank[1][:, j * NS:(j + 1) * NS], v.w2a2[0:64, j * P:(j + 1) * P], lora[0:64, 0, :], start=True, stop=True)
                for j in range(RP):
                    last = nc.tensor.matmul(k.bank[2][:, j * NS:(j + 1) * NS], v.w2a2[64:128, j * P:(j + 1) * P], lora[64:128, 0, :], start=True, stop=True)
                last.then_inc(lw, 1)
                pe.wait_ge(k_sq, 1)
                nc.tensor.matmul(k.bank[3][:, 0:W], k.ones64[:, :], T[5][:, :, :].rearrange("p j t -> p (j t)"), start=True, stop=True).then_inc(k_sum, 1)
                pe.wait_ge(bon, 1)
                nc.tensor.matmul(k.bank[4][:, 0:W], k.ones64[:, :], T[6][:, :, :].rearrange("p j t -> p (j t)"), start=True, stop=True).then_inc(bon_sum, 1)
                pe.wait_ge(vec_made, 1)
                for n in range(12):
                    if n >= 2:
                        pe.wait_ge(tok_off, n - 1)
                    src = six[n // 2]
                    for q in range(4):
                        last = nc.tensor.transpose(k.bank[5 + n % 2][0:NS, q * P:(q + 1) * P], src[:, 4 * (n % 2) + q, :], k.ident[:, :])
                    last.then_inc(tok_turned, 1)

            @block.scalar
            def _(act):
                act.wait_ge(mixed, 1)
                nc.scalar.activation(lora[0:64, 0, :], pm[0:64, 24, :], ACT.Tanh)
                nc.scalar.activation(lora[64:128, 0, :], pm[64:128, 24, :], ACT.Copy)
                nc.scalar.activation(lora[:, 1, :], pm[:, 25, :], ACT.Sigmoid)
                act.drain().then_inc(acted, 1)
                act.wait_ge(sig, 1)
                nc.scalar.activation(T[0][:, :, :], T[0][:, :, :], ACT.Sigmoid)
                nc.scalar.activation(T[2][:, :, :], T[2][:, :, :], ACT.Sigmoid)
                act.drain()
                nc.scalar.activation(T[0][:, :, :], T[0][:, :, :], ACT.Exp, scale=-KAPPA)
                act.drain().then_inc(k_rs, 1)
                act.wait_ge(k_sum, 1)
                nc.scalar.activation(T[5][:, :, :].rearrange("p j t -> p (j t)"), k.bank[3][:, 0:W], ACT.Ln, bias=k.eps[:, 1:2])
                act.drain()
                nc.scalar.activation(T[5][:, :, :], T[5][:, :, :], ACT.Exp, scale=-0.5)
                act.drain().then_inc(k_rs, 1)

            @block.vector
            def _(dve):
                tt, ts = nc.vector.tensor_tensor, nc.vector.tensor_scalar

                def op(f, *a, **kw):
                    f(*a, **kw)
                    dve.drain()
                dve.wait_ge(turned, 1)
                dve.wait_ge(raw_in, 16 * NB)
                op(nc.vector.tensor_copy, ext[:, :, :, 0], k.bank[0][:, 0:RT * NB].rearrange("p (a b) -> p a b", b=NB))
                d4, p4 = [x[:, :, :].rearrange("p a (b t) -> p a b t", t=TS) for x in (d, pm)]
                op(tt, d4, ext[:, :, :, 0:4], ext[:, :, :, 1:5], ALU.subtract)
                op(tt, d[:, :, :], d[:, :, :], k.col["rwkv_mu"].unsqueeze(2).broadcast_to([P, RT, NS]), ALU.mult)
                op(tt, p4, d4, ext[:, :, :, 1:5], ALU.add)
                dve.engine_nop().then_inc(mixed, 1)
                r, kk0, val = pm[:, 0:8, :], pm[:, 8:16, :], pm[:, 16:24, :]
                dve.wait_ge(lw, 1)
                tt(T[0][:, :, :], k.bank[1][:, 0:W].rearrange("p (j t) -> p j t", t=NS), vec("rwkv_w0"), ALU.add)
                op(tt, T[2][:, :, :], k.bank[2][:, 0:W].rearrange("p (j t) -> p j t", t=NS), vec("rwkv_a0"), ALU.add)
                dve.engine_nop().then_inc(sig, 1)
                op(tt, T[1][:, :, :], kk0, vec("rwkv_k_k"), ALU.mult)
                op(tt, T[5][:, :, :], T[1][:, :, :], T[1][:, :, :], ALU.mult)
                dve.engine_nop().then_inc(k_sq, 1)
                dve.wait_ge(k_rs, 1)
                op(ts, T[7][:, :, :], T[2][:, :, :], -1.0, None, ALU.add)
                op(tt, T[7][:, :, :], T[7][:, :, :], vec("rwkv_k_a"), ALU.mult)
                op(ts, T[7][:, :, :], T[7][:, :, :], 1.0, None, ALU.add)
                op(tt, T[7][:, :, :], T[7][:, :, :], kk0, ALU.mult)
                op(tt, T[6][:, :, :], r, T[7][:, :, :], ALU.mult)
                op(tt, T[6][:, :, :], T[6][:, :, :], vec("rwkv_r_k"), ALU.mult)
                dve.engine_nop().then_inc(bon, 1)
                dve.wait_ge(k_rs, 2)
                op(tt, T[1][:, :, :], T[1][:, :, :], T[5][:, :, :], ALU.mult)
                op(tt, T[8][:, :, :], T[1][:, :, :], T[2][:, :, :], ALU.mult)
                op(ts, T[9][:, :, :], T[1][:, :, :], -1.0, None, ALU.mult)
                dve.engine_nop().then_inc(vec_made, 1)
                dve.wait_ge(bon_sum, 1)
                tt(bonus[:, :, :], k.bank[4][:, 0:W].rearrange("p (j t) -> p j t", t=NS), val, ALU.mult)
                for n in range(12):
                    dve.wait_ge(tok_turned, n + 1)
                    nc.vector.tensor_copy(tok[:, (n // 2) * D + (n % 2) * 512:(n // 2) * D + (n % 2 + 1) * 512], k.bank[5 + n % 2][0:NS, :]).then_inc(tok_off, 1)
        rwkv_recur(k, yrow)
        yv, yf = sbk("fin0", [P, W]), sbk("fin1", [P, W])
        T2 = sbk("fin2", [P, W])
        lnw, lnb = sbk("lnw", [P, RP, NS]), sbk("lnb", [P, RP, NS])
        y_turned = S("y_turned")
        with nc.Block() as block:
            @block.tensor
            def _(pe):
                for a in range(RP):
                    last = nc.tensor.transpose(k.bank[0][:, a * NS:(a + 1) * NS], yrow[:, a * P:(a + 1) * P], k.ident[0:NS, 0:NS])
                last.then_inc(y_turned, 1)

            @block.vector
            def _(dve):
                nc.vector.tensor_copy(lnw[:, :, :], k.col["rwkv_ln_w"].unsqueeze(2).broadcast_to([P, RP, NS]))
                nc.vector.tensor_copy(lnb[:, :, :], k.col["rwkv_ln_b"].unsqueeze(2).broadcast_to([P, RP, NS]))
                dve.wait_ge(y_turned, 1)
                nc.vector.tensor_copy(yv[:, :], k.bank[0][:, 0:W])

        def gate(pe):
            for a in range(RP):
                last = nc.tensor.matmul(k.bank[0][:, a * NS:(a + 1) * NS], v.g2[:, a * P:(a + 1) * P], lora[:, 1, :], start=True, stop=True)
            return last
        flat = lambda t: t[:, :, :].rearrange("p a t -> p (a t)")
        rwkv_finish(k, "rxf", yv[:, :], flat(bonus), gate, lambda t0, m: yT[:, :, SEQ:NT], W, flat(lnw), flat(lnb), [yf, T2])


def rwkv_recur(k, yrow):
    nc = k.nc
    S = lambda n: k.sem(f"rr_{n}")
    v_in, s_in, vk_made, vk_used, sw_made, sw_need, y_made, y_out, s_out, back = (S("v_in"), S("s_in"), S("vk_made"), S("vk_used"), S("sw_made"),
                                                                                S("sw_need"), S("y_made"), S("y_out"), S("s_out"), S("back"))
    N = 64
    with ExitStack() as ctx:
        def sb(name, shape):
            return ctx.enter_context(nc.sbuf_tensor(f"rr_{name}", shape, F32))
        vt, yv, sa = sb("vec", [P, TS, 6, N]), sb("y", [P, TS, N]), sb("sa", [P, N])
        tmp = sb("tmp", [P, N, N])
        st = sb("state", [P, N, N])
        vk, sw = [k.ring[:, i, :].rearrange("p (i j) -> p i j", j=N) for i in range(2)]
        block = ctx.enter_context(nc.Block())

        def row(t, a):
            return vt[:, t, a, :].unsqueeze(1).broadcast_to([P, N, N])

        def colv(x):
            return x.unsqueeze(2).broadcast_to([P, N, N])

        @block.sync
        def _(sp):
            for b in range(NB):
                sp.dma_start(vt[16 * b:16 * b + 16, :, :, :], k.vec_dram[TS * b:TS * b + TS].rearrange("t a (h n) -> h t a n", h=16)).then_inc(v_in, 16)
            sp.dma_start(st[:, :, :], k.w["state_rwkv"][0].rearrange("b h i j -> (b h) i j")).then_inc(s_in, 16)
            sp.wait_ge(y_made, 1)
            for b in range(NB):
                sp.dma_start(k.yv_dram[TS * b:TS * b + TS, :].rearrange("t (h n) -> h t n", h=16), yv[16 * b:16 * b + 16, :, :]).then_inc(y_out, 16)
            sp.dma_start(k.out["rwkv_sample"][0].rearrange("b h i j -> (b h) i j"), st[:, :, :]).then_inc(s_out, 16)
            sp.wait_ge(y_out, 16 * NB)
            sp.dma_start(yrow[:, :], k.yv_dram).then_inc(back, 16)
            sp.wait_ge(back, 16)
            sp.wait_ge(s_out, 16)

        @block.gpsimd
        def _(pool):
            pool.wait_ge(v_in, 16 * NB)
            pool.wait_ge(s_in, 16)
            for t in range(TS):
                if t:
                    pool.wait_ge(sw_need, t)
                pool.tensor_tensor(sw, st[:, :, :], row(t, RX_W), ALU.mult).then_inc(sw_made, 1)
                if t:
                    pool.wait_ge(vk_used, t)
                pool.tensor_tensor(vk, colv(vt[:, t, RX_V, :]), row(t, RX_K), ALU.mult).then_inc(vk_made, 1)

        @block.vector
        def _(dve):
            tt = nc.vector.tensor_tensor
            dve.wait_ge(v_in, 16 * NB)
            dve.wait_ge(s_in, 16)
            for t in range(TS):
                tt(tmp[:, :, :], st[:, :, :], row(t, RX_A), ALU.mult)
                dve.drain()
                nc.vector.reduce_sum(sa[:, :], tmp[:, :, :], AX.X)
                dve.drain()
                tt(tmp[:, :, :], colv(sa[:, :]), row(t, RX_B), ALU.mult)
                dve.wait_ge(sw_made, t + 1)
                dve.drain()
                tt(tmp[:, :, :], tmp[:, :, :], sw, ALU.add)
                dve.wait_ge(vk_made, t + 1)
                dve.drain()
                tt(st[:, :, :], tmp[:, :, :], vk, ALU.add)
                dve.drain().then_inc(sw_need, 1)
                dve.engine_nop().then_inc(vk_used, 1)
                tt(tmp[:, :, :], st[:, :, :], row(t, RX_R), ALU.mult)
                dve.drain()
                nc.vector.reduce_sum(yv[:, t, :], tmp[:, :, :], AX.X)
                dve.drain()
            dve.engine_nop().then_inc(y_made, 1)


RX_R, RX_W, RX_K, RX_V, RX_A, RX_B = range(6)


def rwkv(k, yT):
    nc = k.nc
    v = Kernel()
    with ExitStack() as ctx:
        def sb(name, shape):
            return ctx.enter_context(nc.sbuf_tensor(f"r_{name}", shape, F32))
        v.w2a2, v.g2 = sb("w2a2", [P, D]), sb("g2", [P, D])
        v.lora = sb("lora", [P, 2, SEQ])
        rwkv_lora(k, v)
        rwkv_samples(k, v, yT)
        release(k)
        v.m_in, v.m_cross, v.m_lower, v.m_out = sb("m_in", [P, P]), sb("m_cross", [P, P]), sb("m_lower", [P, P]), sb("m_out", [P, 192])
        v.reset = sb("reset", [P, SEQ // 2])
        rwkv_masks(k, v)
        v.AR, v.B, v.K, v.V = sb("AR", [P, RN, 192]), sb("B", [P, RN, P]), sb("K", [P, RN, P]), k.ring[:, 0, 0:RN * P].rearrange("p (c n) -> p c n", n=P)
        v.N = k.ring[:, 0, RN * P:2 * RN * P].rearrange("p (c n) -> p c n", n=P)
        v.KX = k.ring[:, 1, 0:RN * 192].rearrange("p (c n) -> p c n", n=192)
        v.BR = k.ring[:, 1, RN * 192:RN * 256].rearrange("p (c n) -> p c n", n=RC)
        v.PC, v.ST, v.SD, v.R, v.U = sb("PC", [P, RN]), sb("ST", [P, 2, P]), sb("SD", [P, P]), sb("R", [P, P]), sb("U", [P, P])
        v.bonus = sb("bonus", [P, SEQ])
        arena = sb("arena", [P, 11 * SEQ])
        v.T = [arena[:, i * SEQ:(i + 1) * SEQ] for i in range(8)]
        v.pm = arena[:, 8 * SEQ:11 * SEQ].rearrange("p (i t) -> p i t", i=3)
        v.raw = arena[:, 3 * SEQ:6 * SEQ + 12].rearrange("p (i t) -> p i t", i=3)
        v.inv = []
        for p in range(2):
            x = Kernel()
            m = [arena[:, (p * 10 + i) * 512:(p * 10 + i + 1) * 512].rearrange("p (i n) -> p i n", n=P) for i in range(10)]
            x.A, x.D, x.O, x.A2, x.D2, x.A4, x.D4, x.X, x.G, x.F = m
            v.inv.append(x)
        v.y = v.T[7]
        with nc.Block() as block:
            @block.vector
            def _(dve):
                for t in (v.AR, v.B, v.K, v.V):
                    nc.vector.memset(t[:, :, :], 0.0)
        for j in range(RP):
            rwkv_prepare(k, v, j)
            rwkv_invert(k, v, j)
            rwkv_scan(k, v, j)

            def gate(pe, j=j):
                for i in range(2):
                    last = nc.tensor.matmul(k.bank[i][:, :], v.g2[:, j * P:(j + 1) * P], v.lora[:, 1, i * 512:(i + 1) * 512], start=True, stop=True)
                return last
            rwkv_finish(k, f"rf{j}", v.y, v.bonus[:, :], gate, lambda t0, m, j=j: yT[:, j:j + 1, t0:t0 + m], SEQ,
                        k.col["rwkv_ln_w"][:, j:j + 1], k.col["rwkv_ln_b"][:, j:j + 1], v.T[0:2])
            release(k)


GH = 8
CH = SEQ // P


def mamba_dt(k, m):
    nc = k.nc
    loaded, made, absd, expd, logd = (k.sem("mdt_loaded"), k.sem("mdt_made"), k.sem("mdt_abs"), k.sem("mdt_exp"), k.sem("mdt_log"))
    summed, decayed, weighed, turned = k.sem("mdt_summed"), k.sem("mdt_decayed"), k.sem("mdt_weighed"), k.sem("mdt_turned")
    diag_made, spread, masks, endd = k.sem("mdt_diag"), k.sem("mdt_spread"), k.sem("mdt_masks"), k.sem("mdt_endd")
    w = k.w
    with ExitStack() as ctx:
        def sb(name, shape):
            return ctx.enter_context(nc.sbuf_tensor(name, shape, F32))
        hv = sb("m_head_vecs", [32, 4])
        t0, t1, reset, wT, endT = sb("mdt_a", [32, NT]), sb("mdt_b", [32, NT]), sb("mdt_reset", [32, NT]), sb("mdt_w", [32, NT]), sb("mdt_end", [32, 16])
        diag = sb("mdt_diag_end", [32, CH, 32])
        block = ctx.enter_context(nc.Block())

        @block.sync
        def _(sp):
            for i, n in enumerate(("m_dt_bias", "m_a_log", "m_d")):
                sp.dma_start(hv[:, i:i + 1], w[n][0].rearrange("(h a) -> h a", a=1)).then_inc(loaded, 16)

        @block.gpsimd
        def _(pool):
            pool.wait_ge(masks, 1)
            pool.affine_select(out=m.heads[:, :, :], in_=m.heads[:, :, :], compare_op=ALU.is_equal, fill=0.0, base=0,
                               pattern=[[-1, 32], [0, P]], channel_multiplier=1)
            pool.drain()
            pool.affine_select(out=m.feats[:, :].rearrange("h (a p) -> h a p", p=64), in_=m.feats[:, :].rearrange("h (a p) -> h a p", p=64),
                               compare_op=ALU.is_equal, fill=0.0, base=0, pattern=[[-1, 32], [0, 64]], channel_multiplier=1)
            pool.drain()
            for first, pattern, base, mult in ((True, [[-TS, NB], [0, TS]], 0, 1), (False, [[TS, NB], [0, TS]], TS - 1, -1),
                                               (False, [[TS, NB], [1, TS]], 0, -1)):
                v = m.causal[:, :].rearrange("s (b t) -> s b t", t=TS)
                pool.affine_select(out=v, in_=v, compare_op=ALU.is_ge, fill=0.0, base=base, pattern=pattern, channel_multiplier=mult)
                pool.drain()
            for pattern, base, mult in (([[-TS, NB]], 0, 1), ([[TS, NB]], TS - 1, -1)):
                pool.affine_select(out=m.mine[:, :], in_=m.mine[:, :], compare_op=ALU.is_ge, fill=0.0, base=base, pattern=pattern,
                                   channel_multiplier=mult)
                pool.drain()
            pool.engine_nop().then_inc(made, 1)

        @block.vector
        def _(dve):
            for t in (m.heads[:, :, :], m.feats[:, :], m.causal[:, :], m.mine[:, :]):
                nc.vector.memset(t, 1.0)
            dve.drain().then_inc(masks, 1)
            nc.vector.memset(reset[:, :], 1.0)
            dve.drain()
            nc.vector.memset(reset[:, 0:SEQ].rearrange("h (c t) -> h c t", t=P)[:, :, 0:1], 0.0)
            nc.vector.memset(reset[:, SEQ:NT].rearrange("h (b t) -> h b t", t=TS)[:, :, 0:1], 0.0)
            dve.wait_ge(loaded, 48)
            nc.vector.tensor_scalar(t0[:, :], k.dtT[:, :], hv[:, 0:1], None, ALU.add)
            dve.drain().then_inc(summed, 1)
            nc.vector.tensor_scalar(t0[:, :], t0[:, :], 0.0, None, ALU.max)
            dve.wait_ge(logd, 1)
            dve.drain()
            nc.vector.tensor_tensor(m.dt[:, :], t0[:, :], t1[:, :], ALU.add)
            nc.vector.tensor_scalar(hv[:, 3:4], hv[:, 3:4], -1.0, None, ALU.mult)
            dve.drain()
            nc.vector.tensor_scalar(t0[:, :], m.dt[:, :], hv[:, 3:4], None, ALU.mult)
            dve.drain()
            nc.vector.tensor_tensor_scan(out=m.acum[:, :], data0=reset[:, :], data1=t0[:, :], initial=0.0, op0=ALU.mult, op1=ALU.add)
            dve.drain()
            ac, asm = m.acum[:, 0:SEQ].rearrange("h (c t) -> h c t", t=P), m.acum[:, SEQ:NT].rearrange("h (b t) -> h b t", t=TS)
            nc.vector.tensor_tensor(t0[:, 0:SEQ].rearrange("h (c t) -> h c t", t=P), ac[:, :, P - 1:P].broadcast_to([32, CH, P]), ac, ALU.subtract)
            nc.vector.tensor_tensor(t0[:, SEQ:NT].rearrange("h (b t) -> h b t", t=TS), asm[:, :, TS - 1:TS].broadcast_to([32, NB, TS]), asm,
                                    ALU.subtract)
            nc.vector.tensor_copy(endT[:, 0:8], ac[:, :, P - 1])
            nc.vector.tensor_copy(endT[:, 8:16], asm[:, :, TS - 1])
            dve.drain().then_inc(decayed, 1)
            dve.wait_ge(expd, 2)
            nc.vector.tensor_tensor(wT[:, :], t1[:, :], m.dt[:, :], ALU.mult)
            nc.vector.tensor_tensor(diag[:, :, :], k.ident[0:32, 0:32].unsqueeze(1).broadcast_to([32, CH, 32]),
                                    endT[:, 0:8].unsqueeze(2).broadcast_to([32, CH, 32]), ALU.mult)
            dve.drain().then_inc(weighed, 1)
            dve.wait_ge(turned, 1)
            for i, dst in enumerate((m.dt_t, m.acum_t, m.w_t)):
                nc.vector.tensor_copy(dst[:, 0:CH, :], k.bank[i][:, 0:256].rearrange("p (c h) -> p c h", c=CH))
                nc.vector.tensor_copy(dst[0:NS, CH, :], k.bank[i][0:NS, 256:288])
            nc.vector.tensor_copy(m.end[:, :, :], k.bank[3][:, 0:256].rearrange("p (c h) -> p c h", c=CH))
            nc.vector.tensor_copy(m.d[:, :], k.bank[4][:, 0:MZ])
            nc.vector.tensor_copy(m.end_s[:, :, :], k.bank[5][:, 0:P].rearrange("p (a b) -> p a b", b=NB))
            nc.vector.tensor_copy(m.grow_s[:, :, :], k.bank[6][:, :].rearrange("p (a t) -> p a t", t=NS))

        @block.scalar
        def _(act):
            act.wait_ge(loaded, 48)
            nc.scalar.activation(hv[:, 3:4], hv[:, 1:2], ACT.Exp)
            act.wait_ge(summed, 1)
            nc.scalar.activation(t1[:, :], k.dtT[:, :], ACT.Abs, bias=hv[:, 0:1])
            act.drain()
            nc.scalar.activation(t1[:, :], t1[:, :], ACT.Exp, scale=-1.0)
            act.drain()
            nc.scalar.activation(t1[:, :], t1[:, :], ACT.Ln, bias=1.0)
            act.drain().then_inc(logd, 1)
            act.wait_ge(decayed, 1)
            nc.scalar.activation(t1[:, :], t0[:, :], ACT.Exp)
            nc.scalar.activation(endT[:, :], endT[:, :], ACT.Exp)
            act.drain().then_inc(expd, 2)
            nc.scalar.activation(m.grow[:, :], m.acum[:, SEQ:NT], ACT.Exp)
            act.drain().then_inc(endd, 1)

        @block.tensor
        def _(pe):
            pe.wait_ge(weighed, 1)
            pe.wait_ge(endd, 1)
            pe.wait_ge(made, 1)
            for i, src in enumerate((m.dt, m.acum, wT)):
                for c in range(CH):
                    nc.tensor.transpose(k.bank[i][:, c * 32:(c + 1) * 32], src[:, c * P:(c + 1) * P], k.ident[0:32, 0:32])
                nc.tensor.transpose(k.bank[i][0:NS, 256:288], src[:, SEQ:NT], k.ident[0:32, 0:32])
            nc.tensor.matmul(k.bank[3][:, 0:256], k.ones[0:32, :], diag[:, :, :].rearrange("h c e -> h (c e)"), start=True, stop=True)
            for a in range(MZ):
                f = m.feats[:, a * P:(a + 1) * P]
                nc.tensor.matmul(k.bank[4][:, a:a + 1], f, hv[:, 2:3], start=True, stop=True)
                nc.tensor.matmul(k.bank[5][:, a * NB:(a + 1) * NB], f, endT[:, 8:16], start=True, stop=True)
                last = nc.tensor.matmul(k.bank[6][:, a * NS:(a + 1) * NS], f, m.grow[:, :], start=True, stop=True)
            last.then_inc(turned, 1)


def mamba_samples(k, m, tailT, yT):
    nc = k.nc
    conv_in, conv_turned, padded, convd, silud = (k.sem("ms_conv_in"), k.sem("ms_conv_turned"), k.sem("ms_padded"), k.sem("ms_convd"), k.sem("ms_silud"))
    rows_turned, rows_off, spread, segd, expd, mixed = (k.sem("ms_rows_turned"), k.sem("ms_rows_off"), k.sem("ms_spread"), k.sem("ms_segd"), k.sem("ms_expd"), k.sem("ms_mixed"))
    h_in, h_out = [k.sem(f"ms_h_in{s}") for s in range(2)], [k.sem(f"ms_h_out{s}") for s in range(2)]
    h_turned, h_off, y_done, upd, upd_off, xwb_made = (k.sem("ms_h_turned"), k.sem("ms_h_off"), k.sem("ms_y_done"), k.sem("ms_upd"), k.sem("ms_upd_off"), k.sem("ms_xwb"))
    diag_done = k.sem("ms_diag_done")
    state = k.w["state_ssm"][0].rearrange("b h p n -> b (h p) n")
    out = k.out["ssm_sample"][0].rearrange("b h p n -> b (h p) n")
    with ExitStack() as ctx:
        def sb(name, shape):
            return ctx.enter_context(nc.sbuf_tensor(name, shape, F32))
        pad = sb("ms_pad", [P, MX, NB, 7])
        cv, tmp = sb("ms_cv", [P, MX, NS]), sb("ms_tmp", [P, MX, NS])
        xd, xw, bt = sb("ms_xd", [NS, MW]), sb("ms_xw", [NS, MW]), sb("ms_b", [NS, 512])
        xwb = sb("ms_xwb", [NS, 2, MW])
        crow = xwb[0:3 * NB, :, :].rearrange("r a c -> r (a c)")[:, 0:XBC]
        seg, cb = sb("ms_seg", [NS, 32, NS]), sb("ms_cb", [NS, 4, NS])
        hb, hT = sb("ms_h", [P, 2, MZ, P]), sb("ms_hT", [P, MZ, P])
        ys = sb("ms_y", [P, MZ, NS])
        cw = k.col["m_conv_w"]
        block = ctx.enter_context(nc.Block())

        @block.sync
        def _(sp):
            sp.dma_start(crow[:, :], k.w["state_conv"][0].rearrange("b j c -> (b j) c")).then_inc(conv_in, 16)
            for b in range(NB):
                s = b % 2
                if b >= 2:
                    sp.wait_ge(h_out[s], 16 * (b // 2))
                sp.dma_start(hb[:, s, :, :], state[b].rearrange("(a p) n -> p a n", p=P)).then_inc(h_in[s], 16)
                if b >= 1:
                    sp.wait_ge(upd_off, 4 * b)
                    sp.dma_start(out[b - 1].rearrange("(a p) n -> p a n", p=P), hb[:, 1 - s, :, :]).then_inc(h_out[1 - s], 16)
            sp.wait_ge(upd_off, 4 * NB)
            sp.dma_start(out[NB - 1].rearrange("(a p) n -> p a n", p=P), hb[:, 1, :, :]).then_inc(h_out[1], 16)
            for s in range(2):
                sp.wait_ge(h_out[s], 16 * NB // 2)

        @block.tensor
        def _(pe):
            pe.wait_ge(conv_in, 16)
            for a in range(MX):
                last = nc.tensor.transpose(k.bank[a // 12][:, (a % 12) * 24:(a % 12) * 24 + 24], crow[:, a * P:(a + 1) * P],
                                           k.ident[0:24, 0:24])
            last.then_inc(conv_turned, 1)
            pe.wait_ge(silud, 1)
            for a in range(20):
                last = nc.tensor.transpose(k.bank[2 + a // 4][0:NS, (a % 4) * P:(a % 4 + 1) * P], cv[:, a, :], k.ident[:, :])
            last.then_inc(rows_turned, 1)
            for g in range(4):
                nc.tensor.matmul(k.bank[7][0:NS, g * NS:(g + 1) * NS], cv[:, 16 + g, :], cv[:, 20 + g, :], start=True, stop=True)
            for h in range(32):
                last = nc.tensor.matmul(k.bank[h // 16][0:NS, (h % 16) * NS:(h % 16 + 1) * NS], m.heads[:, h, 0:NS], m.acum[:, SEQ:NT],
                                        start=True, stop=True)
            last.then_inc(spread, 1)
            pe.wait_ge(mixed, 1)
            for h in range(32):
                at = 64 * (h % 2)
                last = nc.tensor.matmul(k.bank[0][at:at + 64, (h // 2) * NS:(h // 2 + 1) * NS], xd[:, h * 64:(h + 1) * 64], seg[:, h, :],
                                        start=True, stop=True)
            last.then_inc(diag_done, 1)
            for b in range(NB):
                pe.wait_ge(h_in[b % 2], 16 * (b // 2 + 1))
                if b >= 1:
                    pe.wait_ge(h_off, 4 * b)
                for g in range(4):
                    if g >= 2:
                        pe.wait_ge(h_off, 4 * b + g - 1)
                    for q in range(4):
                        last = nc.tensor.transpose(k.bank[2 + g % 2][:, q * P:(q + 1) * P], hb[:, b % 2, 4 * g + q, :], k.ident[:, :])
                    last.then_inc(h_turned, 1)
                pe.wait_ge(h_off, 4 * b + 4)
                for a in range(MZ):
                    last = nc.tensor.matmul(k.bank[1][:, a * NS + TS * b:a * NS + TS * b + TS], hT[:, a, :],
                                            cv[:, 20 + a // 4, TS * b:TS * b + TS], start=True, stop=True)
                last.then_inc(y_done, 1)
                pe.wait_ge(xwb_made, b + 1)
                for g in range(4):
                    if b >= 1:
                        pe.wait_ge(upd_off, 4 * (b - 1) + g + 1)
                    for q in range(4):
                        a = 4 * g + q
                        last = nc.tensor.matmul(k.bank[4 + g][:, q * P:(q + 1) * P], xwb[:, b % 2, a * P:(a + 1) * P], bt[:, g * P:(g + 1) * P],
                                                start=True, stop=True)
                    last.then_inc(upd, 1)

        @block.scalar
        def _(act):
            act.wait_ge(convd, 1)
            nc.scalar.activation(cv[:, :, :], tmp[:, :, :], ACT.Silu)
            act.drain().then_inc(silud, 1)
            act.wait_ge(segd, 1)
            nc.scalar.activation(seg[:, :, :], seg[:, :, :], ACT.Exp)
            act.drain().then_inc(expd, 1)

        @block.vector
        def _(dve):
            tt = nc.vector.tensor_tensor
            nc.vector.tensor_copy(pad[:, :, :, 3:7], tailT[:, :, :].rearrange("p a (b t) -> p a b t", t=TS))
            dve.wait_ge(conv_turned, 1)
            for i in range(2):
                nc.vector.tensor_copy(pad[:, 12 * i:12 * i + 12, :, 0:3], k.bank[i][:, 0:288].rearrange("p (a b j) -> p a b j", a=12, b=NB))
            dve.drain()

            def tap(j):
                return pad[:, :, :, j:j + TS], cw[:, j * MX:(j + 1) * MX].unsqueeze(2).unsqueeze(3).broadcast_to([P, MX, NB, TS])

            c4, t4 = cv[:, :, :].rearrange("p a (b t) -> p a b t", t=TS), tmp[:, :, :].rearrange("p a (b t) -> p a b t", t=TS)
            x, wj = tap(0)
            tt(t4, x, wj, ALU.mult)
            dve.drain()
            tt(t4, t4, k.col["m_conv_b"].unsqueeze(2).unsqueeze(3).broadcast_to([P, MX, NB, TS]), ALU.add)
            for j in range(1, 4):
                x, wj = tap(j)
                tt(c4, x, wj, ALU.mult)
                dve.drain()
                tt(t4, t4, c4, ALU.add)
                dve.drain()
            dve.drain().then_inc(convd, 1)
            dve.wait_ge(rows_turned, 1)
            for q in range(4):
                v = k.bank[2 + q][0:NS, :].rearrange("s (h p) -> s h p", p=64)
                for dst, by in ((xd, m.dt_t), (xw, m.w_t)):
                    tt(dst[:, q * 512:(q + 1) * 512].rearrange("s (h p) -> s h p", p=64), v,
                       by[0:NS, CH, 8 * q:8 * q + 8].unsqueeze(2).broadcast_to([NS, 8, 64]), ALU.mult)
            nc.vector.tensor_copy(bt[:, :], k.bank[6][0:NS, :])
            dve.wait_ge(spread, 1)
            tt(cb[:, :, :], k.bank[7][0:NS, 0:4 * NS].rearrange("s (g l) -> s g l", g=4), m.causal[:, :].unsqueeze(1).broadcast_to([NS, 4, NS]), ALU.mult)
            for i in range(2):
                tt(seg[:, 16 * i:16 * i + 16, :], k.bank[i][0:NS, :].rearrange("s (h l) -> s h l", l=NS),
                   m.acum_t[0:NS, CH, 16 * i:16 * i + 16].unsqueeze(2).broadcast_to([NS, 16, NS]), ALU.subtract)
            dve.drain()
            nc.vector.tensor_scalar(seg[:, :, :], seg[:, :, :], 0.0, None, ALU.min)
            dve.drain().then_inc(segd, 1)
            dve.wait_ge(expd, 1)
            for g in range(4):
                tt(seg[:, 8 * g:8 * g + 8, :], seg[:, 8 * g:8 * g + 8, :], cb[:, g, :].unsqueeze(1).broadcast_to([NS, 8, NS]), ALU.mult)
            dve.drain().then_inc(mixed, 1)
            for b in range(NB):
                if b >= 2:
                    dve.wait_ge(upd, 4 * (b - 1))
                nc.vector.tensor_scalar(xwb[:, b % 2, :], xw[:, :], m.mine[:, b:b + 1], None, ALU.mult).then_inc(xwb_made, 1)
                for g in range(4):
                    dve.wait_ge(h_turned, 4 * b + g + 1)
                    if b >= 1:
                        dve.wait_ge(y_done, b)
                    nc.vector.tensor_copy(hT[:, 4 * g:4 * g + 4, :], k.bank[2 + g % 2][:, :].rearrange("p (q n) -> p q n", q=4)).then_inc(h_off, 1)
                for g in range(4):
                    dve.wait_ge(upd, 4 * b + g + 1)
                    for q in range(4):
                        a = 4 * g + q
                        last = nc.vector.scalar_tensor_tensor(out=hb[:, b % 2, a, :], in0=hb[:, b % 2, a, :], scalar=m.end_s[:, a, b:b + 1],
                                                              in1=k.bank[4 + g][:, q * P:(q + 1) * P], op0=ALU.mult, op1=ALU.add)
                    last.then_inc(upd_off, 1)
            dve.wait_ge(diag_done, 1)
            dve.wait_ge(y_done, NB)
            tt(ys[:, :, :], k.bank[1][:, :].rearrange("p (a t) -> p a t", t=NS), m.grow_s[:, :, :], ALU.mult)
            tt(tmp[:, 0:MZ, :], cv[:, 0:MZ, :], m.d[:, :].unsqueeze(2).broadcast_to([P, MZ, NS]), ALU.mult)
            dve.drain()
            tt(ys[:, :, :], ys[:, :, :], tmp[:, 0:MZ, :], ALU.add)
            dve.drain()
            tt(yT[:, :, SEQ:NT], ys[:, :, :], k.bank[0][:, :].rearrange("p (a t) -> p a t", t=NS), ALU.add)


def mamba_group(k, m, g, yT):
    nc = k.nc
    S = lambda n: k.sem(f"mg{g}_{n}")
    in_, convd, silud, z_in = [S(f"in{i}") for i in range(6)], S("convd"), S("silud"), S("z_in")
    turned, rows_off, spread, segd, grown, expd, mixed, cgrown = (S("turned"), S("rows_off"), S("spread"), S("segd"), S("grown"), S("expd"),
                                                                  S("mixed"), S("cgrown"))
    y_done, y_off, st_done, h_done, h_turned, h_copied, h_stored = (S("y_done"), S("y_off"), S("st_done"), S("h_done"), S("h_turned"),
                                                                    S("h_copied"), S("h_stored"))
    zsil, gated, squared, summed, rstd_ready = S("zsil"), S("gated"), S("squared"), S("summed"), S("rstd")
    tiles = [4 * g, 4 * g + 1, 4 * g + 2, 4 * g + 3, 16 + g, 20 + g]
    cw, cb_ = k.col["m_conv_w"], k.col["m_conv_b"]
    with ExitStack() as ctx:
        def sb(name, shape):
            return ctx.enter_context(nc.sbuf_tensor(f"mg{g}_{name}", shape, F32))
        raw, acc, cv = sb("raw", [P, 6, 3 + SEQ]), sb("acc", [P, 2, NT]), sb("cv", [P, 6, SEQ])
        grow, seg = sb("grow", [P, 2, GH, P]), sb("seg", [P, 2, GH, P])
        xd, xw, bt, cb = sb("xd", [P, 2, 512]), sb("xw", [P, 2, 512]), sb("bt", [P, 2, P]), sb("cb", [P, 2, P])
        hT, ht = sb("hT", [P, 512]), sb("ht", [P, 512])
        zb = raw[:, :, :].rearrange("p a t -> p (a t)")[:, 0:4 * NT].rearrange("p (a t) -> p a t", a=4)
        BT, CT = cv[:, 4, :], cv[:, 5, :]
        block = ctx.enter_context(nc.Block())

        @block.sync
        def _(sp):
            for i, a in enumerate(tiles):
                r = R_COLS + MW + a * P
                sp.dma_start(raw[:, i, 3:3 + SEQ], k.proj[r:r + P, 0:SEQ]).then_inc(in_[i], 16)
            sp.wait_ge(convd, 6)
            r = R_COLS + 4 * g * P
            sp.dma_start(zb, k.proj[r:r + 4 * P, :].rearrange("(a p) t -> p a t", p=P)).then_inc(z_in, 16)
            sp.wait_ge(h_copied, 1)
            sp.dma_start(k.out["ssm_prompt"][0, 0, GH * g:GH * g + GH].rearrange("(a h) p n -> (h p) a n", h=2),
                         ht[:, :].rearrange("p (a n) -> p a n", n=P)).then_inc(h_stored, 16)
            sp.wait_ge(h_stored, 16)

        @block.tensor
        def _(pe):
            def rows(c):
                t = slice(c * P, (c + 1) * P)
                if c >= 1:
                    pe.wait_ge(rows_off, c)
                for q in range(4):
                    nc.tensor.transpose(k.bank[0][:, q * P:(q + 1) * P], cv[:, q, t], k.ident[:, :])
                nc.tensor.transpose(k.bank[1][:, 0:P], BT[:, t], k.ident[:, :])
                nc.tensor.matmul(k.bank[1][:, P:2 * P], BT[:, t], CT[:, t], start=True, stop=True).then_inc(turned, 1)
                if c >= 1:
                    pe.wait_ge(segd, c)
                for h in range(GH):
                    last = nc.tensor.matmul(k.bank[2 + h // 4][:, (h % 4) * P:(h % 4 + 1) * P], m.heads[:, GH * g + h, :], m.acum[:, t],
                                            start=True, stop=True)
                last.then_inc(spread, 1)

            pe.wait_ge(silud, 6)
            rows(0)
            for c in range(CH):
                if c + 1 < CH:
                    rows(c + 1)
                s = c % 2
                pe.wait_ge(mixed, c + 1)
                pe.wait_ge(cgrown, c + 1)
                if c >= 1:
                    pe.wait_ge(h_done, c)
                    pe.wait_ge(y_off, c)
                for h in range(GH):
                    o = k.bank[4][64 * (h % 2):64 * (h % 2) + 64, (h // 2) * P:(h // 2 + 1) * P]
                    last = nc.tensor.matmul(o, xd[:, s, h * 64:(h + 1) * 64], seg[:, s, h, :], start=True, stop=c == 0)
                    if c:
                        last = nc.tensor.matmul(o, hT[:, h * 64:(h + 1) * 64], grow[:, s, h, :], start=False, stop=True)
                last.then_inc(y_done, 1)
                nc.tensor.matmul(k.bank[5][:, :], bt[:, s, :], xw[:, s, :], start=True, stop=True).then_inc(st_done, 1)
            pe.wait_ge(h_done, CH)
            for q in range(4):
                last = nc.tensor.transpose(k.bank[0][:, q * P:(q + 1) * P], hT[:, q * P:(q + 1) * P], k.ident[:, :])
            last.then_inc(h_turned, 1)
            for q in range(4):
                pe.wait_ge(squared, q + 1)
                for i, (t0, n) in enumerate(chunks3()):
                    last = nc.tensor.matmul(k.bank[5 + i][:, 0:n], k.ones[:, :], acc[:, q % 2, t0:t0 + n], start=q == 0, stop=q == 3)
                last.then_inc(summed, 1)

        @block.vector
        def _(dve):
            tt, stt = nc.vector.tensor_tensor, nc.vector.scalar_tensor_tensor
            nc.vector.memset(raw[:, :, 0:3], 0.0)
            nc.vector.memset(hT[:, :], 0.0)
            dve.drain()
            for i, a in enumerate(tiles):
                dve.wait_ge(in_[i], 16)
                if i >= 2:
                    dve.wait_ge(silud, i - 1)
                o = acc[:, i % 2, 0:SEQ]
                nc.vector.tensor_scalar(o, raw[:, i, 0:SEQ], cw[:, a:a + 1], cb_[:, a:a + 1], ALU.mult, ALU.add)
                dve.drain()
                for j in range(1, 4):
                    last = stt(out=o, in0=raw[:, i, j:j + SEQ], scalar=cw[:, j * MX + a:j * MX + a + 1], in1=o, op0=ALU.mult, op1=ALU.add)
                    if j < 3:
                        dve.drain()
                last.then_inc(convd, 1)

            def rows(c):
                s = c % 2
                dve.wait_ge(turned, c + 1)
                v = k.bank[0][:, :].rearrange("s (h p) -> s h p", p=64)
                for dst, by in ((xd, m.dt_t), (xw, m.w_t)):
                    tt(dst[:, s, :].rearrange("s (h p) -> s h p", p=64), v, by[:, c, GH * g:GH * g + GH].unsqueeze(2).broadcast_to([P, GH, 64]), ALU.mult)
                nc.vector.tensor_copy(bt[:, s, :], k.bank[1][:, 0:P])
                tt(cb[:, s, :], k.bank[1][:, P:2 * P], k.upper[:, :], ALU.mult).then_inc(rows_off, 1)
                dve.wait_ge(grown, c + 1)
                for h in range(GH):
                    last = nc.vector.tensor_scalar(seg[:, s, h, :], k.bank[2 + h // 4][:, (h % 4) * P:(h % 4 + 1) * P],
                                                   m.acum_t[:, c, GH * g + h:GH * g + h + 1], 0.0, ALU.subtract, ALU.min)
                last.then_inc(segd, 1)

            rows(0)
            for c in range(CH):
                s = c % 2
                if c + 1 < CH:
                    rows(c + 1)
                dve.wait_ge(expd, c + 1)
                tt(seg[:, s, :, :], seg[:, s, :, :], cb[:, s, :].unsqueeze(1).broadcast_to([P, GH, P]), ALU.mult).then_inc(mixed, 1)
                tt(ht[:, :].rearrange("p (h q) -> p h q", q=64), hT[:, :].rearrange("p (h q) -> p h q", q=64),
                   m.end[:, c, GH * g:GH * g + GH].unsqueeze(2).broadcast_to([P, GH, 64]), ALU.mult)
                dve.wait_ge(y_done, c + 1)
                for q in range(4):
                    last = stt(out=yT[:, 4 * g + q, c * P:(c + 1) * P], in0=cv[:, q, c * P:(c + 1) * P], scalar=m.d[:, 4 * g + q:4 * g + q + 1],
                               in1=k.bank[4][:, q * P:(q + 1) * P], op0=ALU.mult, op1=ALU.add)
                last.then_inc(y_off, 1)
                dve.wait_ge(st_done, c + 1)
                dve.drain()
                tt(hT[:, :], ht[:, :], k.bank[5][:, :], ALU.add).then_inc(h_done, 1)
                dve.drain()
            dve.wait_ge(h_turned, 1)
            nc.vector.tensor_copy(ht[:, :], k.bank[0][:, :]).then_inc(h_copied, 1)
            for q in range(4):
                dve.wait_ge(zsil, q + 1)
                tt(yT[:, 4 * g + q, :], yT[:, 4 * g + q, :], zb[:, q, :], ALU.mult).then_inc(gated, 1)
            dve.wait_ge(rstd_ready, 1)
            for q in range(4):
                a = 4 * g + q
                stt(out=yT[:, a, :], in0=yT[:, a, :], scalar=k.col["m_norm"][:, a:a + 1], in1=acc[:, 0, :], op0=ALU.mult, op1=ALU.mult)

        @block.scalar
        def _(act):
            for i in range(6):
                act.wait_ge(convd, i + 1)
                nc.scalar.activation(cv[:, i, :], acc[:, i % 2, 0:SEQ], ACT.Silu).then_inc(silud, 1)

            def grow_and_exp(c):
                s = c % 2
                act.wait_ge(spread, c + 1)
                if c >= 2:
                    act.wait_ge(y_done, c - 1)
                for i in range(2):
                    last = nc.scalar.activation(grow[:, s, 4 * i:4 * i + 4, :], k.bank[2 + i][:, :].rearrange("p (h l) -> p h l", h=4), ACT.Exp)
                last.then_inc(grown, 1)
                act.wait_ge(segd, c + 1)
                nc.scalar.activation(seg[:, s, :, :], seg[:, s, :, :], ACT.Exp).then_inc(expd, 1)
            for c in range(CH):
                grow_and_exp(c)
            act.wait_ge(z_in, 16)
            for q in range(4):
                nc.scalar.activation(zb[:, q, :], zb[:, q, :], ACT.Silu).then_inc(zsil, 1)
            for q in range(4):
                act.wait_ge(gated, q + 1)
                if q >= 2:
                    act.wait_ge(summed, q - 1)
                nc.scalar.activation(acc[:, q % 2, :], yT[:, 4 * g + q, :], ACT.Square).then_inc(squared, 1)
            act.wait_ge(summed, 4)
            for i, (t0, n) in enumerate(chunks3()):
                nc.scalar.activation(acc[:, 0, t0:t0 + n], k.bank[5 + i][:, 0:n], ACT.Ln, bias=k.eps[:, 0:1], scale=1.0 / 512)
            act.drain()
            nc.scalar.activation(acc[:, 0, :], acc[:, 0, :], ACT.Exp, scale=-0.5).then_inc(rstd_ready, 1)

        @block.gpsimd
        def _(pool):
            for c in range(CH):
                pool.wait_ge(grown, c + 1)
                pool.tensor_tensor(grow[:, c % 2, :, :], grow[:, c % 2, :, :], CT[:, c * P:(c + 1) * P].unsqueeze(1).broadcast_to([P, GH, P]),
                                   ALU.mult).then_inc(cgrown, 1)


def mamba(k, yT):
    nc = k.nc
    m = Kernel()
    with ExitStack() as ctx:
        def sb(name, shape):
            return ctx.enter_context(nc.sbuf_tensor(f"m_{name}", shape, F32))
        m.heads = k.ring[0:32, 0, :].rearrange("h (e l) -> h e l", l=P)
        m.feats = k.ring[0:32, 1, 0:MW]
        m.dt, m.acum = k.ring[0:32, 1, MW:MW + NT], sb("acum", [32, NT])
        m.causal, m.mine, m.grow = sb("causal", [NS, NS]), sb("mine", [NS, NB]), sb("grow", [32, NS])
        m.dt_t, m.acum_t, m.w_t = sb("dt_t", [P, CH + 1, 32]), sb("acum_t", [P, CH + 1, 32]), sb("w_t", [P, CH + 1, 32])
        m.end, m.d, m.end_s, m.grow_s = sb("end", [P, CH, 32]), sb("d", [P, MZ]), sb("end_s", [P, MZ, NB]), sb("grow_s", [P, MZ, NS])
        mamba_dt(k, m)
        with nc.sbuf_tensor("m_tail", [P, MX, NS], F32) as tailT:
            move(k, "m_tail", tailT[:, :, :], k.proj[R_COLS + MW:ROWS, SEQ:NT].rearrange("(a p) t -> p a t", p=P))
            mamba_samples(k, m, tailT, yT)
        release(k)
        for g in range(4):
            mamba_group(k, m, g, yT)
        release(k)


def gated(k, tag, W, y, gate, merged):
    with ExitStack() as ctx:
        gemm(k, tag, [Part(W, Pair(k, ctx, f"{tag}_y"), KD, 4, Gate(k, y, merged), raw=y, fetch=(y, gate))], chunks3())


def layer(k, ctx):
    nc, w = k.nc, k.w

    def act(name, scope, tiles=KD):
        return scope.enter_context(nc.sbuf_tensor(name, [P, tiles, NT], F32))

    with ExitStack() as s:
        xnT = act("xnT", s)
        with ExitStack() as s1:
            hT = act("hT", s1)
            load_tokens(k, "x", w["x_prompt"][0], w["x_sample"].rearrange("b t d -> (b t) d"), hT)
            norm(k, "mixpre", hT, xnT, k.col["norm_mix_pre"], chunks3())
            move(k, "h_out", k.h_dram, hT[:, :, :])
            move(k, "xn_out", k.xn_dram, xnT[:, :, :])
        project_to_dram(k, xnT)
        with nc.sbuf_tensor("tailT", [P, ROWS // P, TAIL], F32) as tailT:
            tails(k, tailT)
    release(k)
    with ExitStack() as s:
        both = act("both", s, MZ)
        merged, yT = both[:, 0:KD, :], both[:, KD:MZ, :]
        gates = k.gates.rearrange("(g a p) t -> g p a t", g=3, p=P)
        mamba(k, both)
        with ExitStack() as s1:
            pair, W = Pair(k, s1, "mamba_y"), w["w_out_mamba"][0]
            gemm(k, "gm", [Part(W[0:D, :], pair, KD, 4, Accumulate(k, merged, True), raw=merged),
                           Part(W[D:MW, :], pair, KD, 4, Accumulate(k, merged, False, yT), raw=yT, fetch=(yT, gates[2]))], chunks3())
        release(k)
        s5(k, yT)
        with ExitStack() as s1:
            gemm(k, "glu", [Part(w["s5_w_glu"][0], Pair(k, s1, "glu_x"), KD, 4, raw=yT,
                                 hooks=StoreRows(k, "glu", k.glu, k.ring[:, 1, 0:2 * NT].rearrange("p (s t) -> p s t", s=2), ACT.Sigmoid))], chunks3())
        with ExitStack() as s1:
            g = act("s5_glu", s1)
            move(k, "glu_back", g[:, :, :], k.glu.rearrange("(a p) t -> p a t", p=P))
            with nc.Block() as block:
                @block.vector
                def _(dve):
                    nc.vector.tensor_tensor(yT, yT, g[:, :, :], ALU.mult)
        gated(k, "gs", w["w_out_s5"][0], yT, gates[1], merged)
        release(k)
        rwkv(k, yT)
        gated(k, "gr", w["w_out_rwkv"][0], yT, gates[0], merged)
        product(k, "mix", w["w_out"][0], merged, yT)
        move(k, "h_back", merged, k.h_dram)
        norm(k, "mixpost", yT, yT, k.col["norm_mix_post"], chunks3(), residual=merged)
        release(k)
        attention(k, both)
        release(k)
    mlp_sublayer(k)


def build(nc, ins, outs):
    k = Kernel()
    k.nc, k.out = nc, outs
    w = {n: ap for n, ap in ins.items()}
    with ExitStack() as ctx:
        def sb(name, shape):
            return ctx.enter_context(nc.sbuf_tensor(name, shape, F32))

        k.sems = []
        k.sem = lambda name: k.sems.append(nc.alloc_semaphore(name)) or k.sems[-1]
        k.bank = [ctx.enter_context(nc.psum_tensor(f"bank{i}", [P, 512], F32)) for i in range(8)]
        k.ident, k.ones, k.ones64, k.upper = sb("ident", [P, P]), sb("ones", [P, P]), sb("ones64", [P, P]), sb("upper", [P, P])
        k.eps = sb("eps", [P, 4])
        k.ring = sb("ring", [P, 2, RING])
        k.dtT = sb("dtT", [32, NT])
        k.w_in = w["w_in"][0]
        k.proj = nc.dram_tensor("proj_scratch", [ROWS, NT], F32).ap()
        k.gates = nc.dram_tensor("gates_scratch", [3 * D, NT], F32).ap()
        k.glu = nc.dram_tensor("glu_scratch", [D, NT], F32).ap()
        k.h_dram = nc.dram_tensor("h_scratch", [P, KD, NT], F32).ap()
        k.vec_dram = nc.dram_tensor("vec_scratch", [NS, 6, D], F32).ap()
        k.yv_dram = nc.dram_tensor("yv_scratch", [NS, D], F32).ap()
        k.xn_dram = nc.dram_tensor("xn_scratch", [P, KD, NT], F32).ap()

        k.vec_rows, k.vec_used, cols = [], [0, 0, 0], {}
        vecs = [[(n, w[n][0]) for n in ("norm_mix_pre", "norm_mix_post", "norm_xa_pre", "norm_xa_post", "norm_mlp_pre",
                                        "norm_mlp_post", "norm_mem", "rwkv_w0", "rwkv_a0", "rwkv_k_k", "rwkv_k_a",
                                        "rwkv_ln_w", "rwkv_ln_b")],
                [("rwkv_mu", w["rwkv_mu"][0]), ("m_norm", w["m_norm"][0]), ("m_conv_b", w["m_conv_b"][0]),
                 ("rwkv_r_k", w["rwkv_r_k"][0].rearrange("h n -> (h n)"))],
                [("m_conv_w", w["m_conv_w"][0].rearrange("j n -> (j n)"))]]
        for tile, members in enumerate(vecs):
            for name, ap in members:
                r = ap.shape[0] // P
                k.vec_rows.append((name, tile, k.vec_used[tile], ap.rearrange("(r p) -> r p", p=P)))
                cols[name] = (tile * P + k.vec_used[tile], r)
                k.vec_used[tile] += r
        k.vec = sb("vec", [P, 3 * P])
        k.col = {n: k.vec[:, c:c + r] for n, (c, r) in cols.items()}
        k.w = w

        constants(k)
        layer(k, ctx)


OUT_NAMES = ["y_prompt", "y_sample", "mem_k_prompt", "mem_v_prompt", "rwkv_prompt", "rwkv_shift_prompt", "s5_re_prompt",
             "s5_im_prompt", "conv_prompt", "ssm_prompt", "rwkv_sample", "rwkv_shift_sample", "s5_re_sample",
             "s5_im_sample", "conv_sample", "ssm_sample"]
OUT_SHAPES = [(1, SEQ, D), (NB, TS, D), (1, 1, 256, 4, 256), (1, 1, 256, 4, 256), (1, 1, 16, 64, 64), (1, 1, R_COLS),
              (1, 1, 64, 64), (1, 1, 64, 64), (1, 1, 3, XBC), (1, 1, 32, 64, P), (1, NB, 16, 64, 64), (1, NB, R_COLS),
              (1, NB, 64, 64), (1, NB, 64, 64), (1, NB, 3, XBC), (1, NB, 32, 64, P)]


def kernel(**inputs):
    import numpy as _np
    import concourse.bacc as _bacc
    from concourse import mybir as _mybir
    from concourse.bass_utils import run_bass_kernel_spmd as _run

    nc = _bacc.Bacc("TRN2", target_bir_lowering=False, num_devices=1)
    arrays, ins, outs = {}, {}, {}
    for name, value in inputs.items():
        a = _np.ascontiguousarray(value)
        arrays[f"in_{name}_dram"] = a
        ins[name] = nc.dram_tensor(f"in_{name}_dram", a.shape, _mybir.dt.from_np(a.dtype), kind="ExternalInput").ap()
    for name, shape in zip(OUT_NAMES, OUT_SHAPES):
        outs[name] = nc.dram_tensor(f"out_{name}_dram", shape, _mybir.dt.from_np(_np.dtype("float32")), kind="ExternalOutput").ap()
    build(nc, ins, outs)
    r = _run(nc, [arrays], core_ids=[0])
    return tuple(r.results[0][f"out_{n}_dram"] for n in OUT_NAMES)
```
